# Optimizing a Trainium2 kernel written in Bass

```python
import math, functools
import jax, jax.numpy as jnp
from jax import lax
import numpy as np

D_MODEL = 1024
BATCH = 1
SEQ = 512
DEPTH = 2
DEC_BATCH = 8
DEC_SEQ = 8
PAST_LEN = 256
PAGE_SIZE = 128

D_ATTN = D_MODEL // 2
ATTN_HEAD_DIM = 64
N_ATTN_HEADS = D_ATTN // ATTN_HEAD_DIM
ATTN_SCALE = ATTN_HEAD_DIM ** -0.5
D_REC = D_MODEL - D_ATTN
REC_EXPAND = 128
N_REC_HEADS = D_REC // REC_EXPAND
REC_DV = D_REC // N_REC_HEADS
REC_CHUNK = 64
D_FF = 4 * D_MODEL
DILATED_PATTERNS = ((128, 1), (512, 4), (2048, 16))
MAX_WINDOW = max(w for w, _ in DILATED_PATTERNS)
BAND_BLOCK = 128
NUM_BUCKETS = 32
MAX_DISTANCE = MAX_WINDOW
RMS_EPS = 1e-6
NEG_INF = -1e30
MIN_FORGET = 1e-30
IN_COLS = 4 * D_REC + 3 * D_ATTN

kernel_name = "hymba_hgrn2_dilated_swa_decoder_step"

def rms_norm(x, g):
    xf = x.astype(jnp.float32)
    y = xf * lax.rsqrt(jnp.mean(xf * xf, axis=-1, keepdims=True) + RMS_EPS)
    return (y * g.astype(jnp.float32)).astype(x.dtype)

def rel_bucket(dist):
    exact = NUM_BUCKETS // 2
    d = jnp.maximum(dist, exact).astype(jnp.float32)
    large = exact + (jnp.log(d / exact) / math.log(MAX_DISTANCE / exact) * (NUM_BUCKETS - exact)).astype(jnp.int32)
    large = jnp.minimum(large, NUM_BUCKETS - 1)
    return jnp.where(dist < exact, dist, large)

def gated_linear_recurrence(q, k, v, logf, s0, chunk):
    B, T, H, DK = q.shape
    DV = v.shape[-1]
    n = T // chunk

    def blocks(a):
        return a.reshape(B, n, chunk, H, a.shape[-1]).transpose(1, 0, 3, 2, 4)

    causal = jnp.tril(jnp.ones((chunk, chunk), dtype=bool))

    def step(state, inp):
        qc, kc, vc, gc = inp
        b = jnp.cumsum(gc, axis=2)
        diff = b[:, :, :, None, :] - b[:, :, None, :, :]
        decay = jnp.exp(jnp.where(causal[:, :, None], diff, NEG_INF))
        scores = jnp.einsum('bhtsk,bhsk->bhts', qc[:, :, :, None, :] * decay, kc)
        out = (jnp.einsum('bhts,bhsv->bhtv', scores, vc)
               + jnp.einsum('bhtk,bhkv->bhtv', qc * jnp.exp(b), state))
        b_last = b[:, :, -1:, :]
        state = (jnp.exp(b_last[:, :, 0, :, None]) * state
                 + jnp.einsum('bhsk,bhsv->bhkv', kc * jnp.exp(b_last - b), vc))
        return state, out

    s_final, out = lax.scan(step, s0, (blocks(q), blocks(k), blocks(v), blocks(logf)))
    out = out.transpose(1, 0, 3, 2, 4).reshape(B, T, H, DV)
    return out, s_final

def hgrn2_mixer(q_in, f_in, i_in, g_in, lb, g_norm, s0):
    B, T, _ = q_in.shape
    heads = lambda a: a.reshape(B, T, N_REC_HEADS, -1).astype(jnp.float32)
    z = heads(f_in)
    lbh = lb.reshape(N_REC_HEADS, REC_EXPAND)
    f = lbh + (1.0 - lbh) * jax.nn.sigmoid(z)
    logf = jnp.log(jnp.maximum(f, MIN_FORGET))
    k = (1.0 - lbh) * jax.nn.sigmoid(-z)
    q = jax.nn.silu(heads(q_in))
    v = heads(i_in)
    chunk = REC_CHUNK if T % REC_CHUNK == 0 else T
    o, s_final = gated_linear_recurrence(q, k, v, logf, s0, chunk)
    o = rms_norm(o, g_norm.reshape(N_REC_HEADS, REC_DV)) * jax.nn.silu(heads(g_in))
    return o.reshape(B, T, D_REC).astype(q_in.dtype), s_final

def dilated_band_attention(q, k, v, rel_bias, window, dil):
    B, S, H, Dh = q.shape
    taps = window // dil
    L = S // dil
    nb = -(-L // BAND_BLOCK)
    Lp = nb * BAND_BLOCK
    N = B * dil

    def to_sub(a, front):
        a = a.reshape(B, L, dil, H, Dh).transpose(0, 2, 1, 3, 4).reshape(N, L, H, Dh)
        return jnp.pad(a, ((0, 0), (front, Lp - L), (0, 0), (0, 0)))

    def band(a):
        ap = to_sub(a, BAND_BLOCK)
        prev = ap[:, :Lp].reshape(N, nb, BAND_BLOCK, H, Dh)
        cur = ap[:, BAND_BLOCK:].reshape(N, nb, BAND_BLOCK, H, Dh)
        return jnp.concatenate([prev, cur], axis=2)

    qb = to_sub(q, 0).reshape(N, nb, BAND_BLOCK, H, Dh)
    kb, vb = band(k), band(v)
    scores = jnp.einsum('nbqhd,nbkhd->nbhqk', qb, kb, preferred_element_type=jnp.float32) * ATTN_SCALE
    qi = jnp.arange(BAND_BLOCK)[:, None]
    ki = jnp.arange(2 * BAND_BLOCK)[None, :]
    tap = qi + BAND_BLOCK - ki
    bias = rel_bias[rel_bucket(jnp.maximum(tap, 0) * dil)]
    key_idx = jnp.arange(nb)[:, None, None] * BAND_BLOCK + ki[None] - BAND_BLOCK
    valid = ((tap >= 0) & (tap <= taps))[None] & (key_idx >= 0)
    scores = jnp.where(valid[None, :, None],
                       scores + jnp.transpose(bias, (2, 0, 1)).astype(jnp.float32)[None, None], NEG_INF)
    m = jnp.max(scores, axis=-1, keepdims=True)
    p = jnp.exp(scores - m)
    den = jnp.sum(p, axis=-1)
    o = jnp.einsum('nbhqk,nbkhd->nbqhd', p, vb.astype(jnp.float32)) / jnp.transpose(den, (0, 1, 3, 2))[..., None]
    lse = jnp.transpose(m[..., 0] + jnp.log(den), (0, 1, 3, 2))

    def from_sub(a):
        a = a.reshape(N, Lp, *a.shape[3:])[:, :L]
        a = a.reshape(B, dil, L, *a.shape[2:])
        return jnp.swapaxes(a, 1, 2).reshape(B, S, *a.shape[3:])

    return from_sub(o), from_sub(lse)

def dilated_gather_attention(q, k_all, v_all, rel_bias, window, dil):
    T = q.shape[1]
    n_past = k_all.shape[1] - T
    taps = window // dil
    j = jnp.arange(taps + 1)
    idx = n_past + jnp.arange(T)[:, None] - j[None, :] * dil
    valid = idx >= 0
    idx = jnp.maximum(idx, 0)
    kg = k_all[:, idx]
    vg = v_all[:, idx]
    bias = rel_bias[rel_bucket(j * dil)]
    scores = (jnp.einsum('bthd,btjhd->bthj', q, kg, preferred_element_type=jnp.float32) * ATTN_SCALE
              + bias.T.astype(jnp.float32))
    scores = jnp.where(valid[:, None, :], scores, NEG_INF)
    m = jnp.max(scores, axis=-1, keepdims=True)
    p = jnp.exp(scores - m)
    den = jnp.sum(p, axis=-1)
    o = jnp.einsum('bthj,btjhd->bthd', p, vg.astype(jnp.float32)) / den[..., None]
    return o, m[..., 0] + jnp.log(den)

def mix_patterns(outs, lses):
    w = jax.nn.softmax(jnp.stack(lses, axis=0), axis=0)
    return jnp.einsum('pbth,pbthd->bthd', w, jnp.stack(outs, axis=0))

def prompt_attention(q, k, v, rel_bias):
    res = [dilated_band_attention(q, k, v, rel_bias, w, d) for w, d in DILATED_PATTERNS]
    return mix_patterns([r[0] for r in res], [r[1] for r in res])

def sample_attention(q, k, v, ck, cv, rel_bias):
    k_all = jnp.concatenate([ck.astype(k.dtype), k], axis=1)
    v_all = jnp.concatenate([cv.astype(v.dtype), v], axis=1)
    res = [dilated_gather_attention(q, k_all, v_all, rel_bias, w, d) for w, d in DILATED_PATTERNS]
    return mix_patterns([r[0] for r in res], [r[1] for r in res])

def trunk_layer(x, attn_fn, s0, lb, w_in, w_out, w_up, w_down,
                g_mix_pre, g_mix_post, g_mlp_pre, g_mlp_post, g_rec_out, g_attn_out):
    B, T, _ = x.shape
    h = rms_norm(x, g_mix_pre)
    proj = jnp.einsum('btd,dc->btc', h, w_in)
    splits = list(np.cumsum([D_REC] * 4 + [D_ATTN] * 2))
    q_r, f_r, i_r, g_r, q_a, k_a, v_a = jnp.split(proj, splits, axis=-1)
    rec_out, s_new = hgrn2_mixer(q_r, f_r, i_r, g_r, lb, g_rec_out, s0)
    ah = lambda a: a.reshape(B, T, N_ATTN_HEADS, ATTN_HEAD_DIM)
    q_a, k_a, v_a = ah(q_a), ah(k_a), ah(v_a)
    attn = attn_fn(q_a, k_a, v_a)
    attn = rms_norm(attn, g_attn_out.reshape(N_ATTN_HEADS, ATTN_HEAD_DIM)).reshape(B, T, D_ATTN).astype(x.dtype)
    mixed = jnp.einsum('btc,cd->btd', jnp.concatenate([rec_out, attn], axis=-1), w_out)
    x = x + rms_norm(mixed, g_mix_post)
    h = rms_norm(x, g_mlp_pre)
    u = jnp.square(jax.nn.relu(jnp.einsum('btd,df->btf', h, w_up)))
    x = x + rms_norm(jnp.einsum('btf,fd->btd', u, w_down), g_mlp_post)
    return x, s_new, k_a, v_a

def setup_inputs(seed: int = 0) -> dict:
    key = jax.random.key(seed)
    ks = jax.random.split(key, 18)
    f32 = jnp.float32
    nrm = lambda k, shape, scale: scale * jax.random.normal(k, shape, f32)
    win = min(MAX_WINDOW, PAST_LEN)
    return {
        "x_prompt": nrm(ks[0], (BATCH, SEQ, D_MODEL), 1.0),
        "x_sample": nrm(ks[1], (DEC_BATCH, DEC_SEQ, D_MODEL), 1.0),
        "state_hgrn": nrm(ks[2], (DEPTH, DEC_BATCH, N_REC_HEADS, REC_EXPAND, REC_DV), 0.5),
        "cache_k": nrm(ks[3], (DEPTH, DEC_BATCH, win, N_ATTN_HEADS, ATTN_HEAD_DIM), 1.0),
        "cache_v": nrm(ks[4], (DEPTH, DEC_BATCH, win, N_ATTN_HEADS, ATTN_HEAD_DIM), 1.0),
        "rel_bias": nrm(ks[5], (NUM_BUCKETS, N_ATTN_HEADS), 0.5),
        "lb_raw": nrm(ks[6], (DEPTH, D_REC), 0.5),
        "w_in": nrm(ks[7], (DEPTH, D_MODEL, IN_COLS), D_MODEL ** -0.5),
        "w_out": nrm(ks[8], (DEPTH, D_MODEL, D_MODEL), D_MODEL ** -0.5),
        "w_up": nrm(ks[9], (DEPTH, D_MODEL, D_FF), D_MODEL ** -0.5),
        "w_down": nrm(ks[10], (DEPTH, D_FF, D_MODEL), D_FF ** -0.5),
        "g_mix_pre": 1.0 + nrm(ks[11], (DEPTH, D_MODEL), 0.02),
        "g_mix_post": 1.0 + nrm(ks[12], (DEPTH, D_MODEL), 0.02),
        "g_mlp_pre": 1.0 + nrm(ks[13], (DEPTH, D_MODEL), 0.02),
        "g_mlp_post": 1.0 + nrm(ks[14], (DEPTH, D_MODEL), 0.02),
        "g_rec_out": 1.0 + nrm(ks[15], (DEPTH, D_REC), 0.02),
        "g_attn_out": 1.0 + nrm(ks[16], (DEPTH, D_ATTN), 0.02),
    }

def reference(x_prompt, x_sample, state_hgrn, cache_k, cache_v, rel_bias, lb_raw, w_in, w_out, w_up, w_down,
              g_mix_pre, g_mix_post, g_mlp_pre, g_mlp_post, g_rec_out, g_attn_out):
    lb_soft = jax.nn.softmax(lb_raw.astype(jnp.float32), axis=0)
    lower_bounds = jnp.cumsum(lb_soft, axis=0) - lb_soft[0]
    keep = min(MAX_WINDOW, x_prompt.shape[1])
    p_attn = functools.partial(prompt_attention, rel_bias=rel_bias)
    yp, ys = x_prompt, x_sample
    rec_p, k_p, v_p, rec_s, k_s, v_s = [], [], [], [], [], []
    for l in range(DEPTH):
        lw = (w_in[l], w_out[l], w_up[l], w_down[l], g_mix_pre[l], g_mix_post[l],
              g_mlp_pre[l], g_mlp_post[l], g_rec_out[l], g_attn_out[l])
        s0 = jnp.zeros((yp.shape[0], N_REC_HEADS, REC_EXPAND, REC_DV), jnp.float32)
        yp, sp, kp, vp = trunk_layer(yp, p_attn, s0, lower_bounds[l], *lw)
        rec_p.append(sp)
        k_p.append(kp[:, -keep:])
        v_p.append(vp[:, -keep:])
        s_attn = functools.partial(sample_attention, ck=cache_k[l], cv=cache_v[l], rel_bias=rel_bias)
        ys, ss, ksm, vsm = trunk_layer(ys, s_attn, state_hgrn[l].astype(jnp.float32), lower_bounds[l], *lw)
        rec_s.append(ss)
        k_s.append(ksm)
        v_s.append(vsm)
    return (yp, ys, jnp.stack(rec_p), jnp.stack(k_p), jnp.stack(v_p),
            jnp.stack(rec_s), jnp.stack(k_s), jnp.stack(v_s))


_drawn_inputs = setup_inputs


def setup_inputs(seed=0):
    import zlib

    import numpy as np

    out = dict(_drawn_inputs(seed))
    spreads = {}
    factors = {'g_mix_post': 3.021,
     'g_mlp_pre': 3.179,
     'g_mlp_post': 9.603,
     'g_rec_out': 18.788,
     'g_attn_out': 10.838}
    for name, (base, spread) in spreads.items():
        noise = np.random.default_rng([zlib.crc32(name.encode()), seed]).standard_normal(out[name].shape)
        drawn = base * np.exp(spread * noise) if base else spread * noise
        out[name] = __import__('jax').numpy.asarray(drawn.astype(out[name].dtype))
    for name, factor in factors.items():
        out[name] = (out[name] * factor).astype(out[name].dtype)
    return out
```

```python
from contextlib import ExitStack, contextmanager

import numpy as np
import concourse.bass as bass
from concourse import mybir

F32 = mybir.dt.float32
F32R = mybir.dt.float32r
U8 = mybir.dt.uint8
ALU = mybir.AluOpType
ACT = mybir.ActivationFunctionType
AX = mybir.AxisListType

P = 128
DEPTH, D, FF = 2, 1024, 4096
TP, NB, TB = 512, 8, 8
TS = NB * TB
TT = TP + TS
HT = TT // 2
KC = D // P
HR, HA, DH = 4, 8, 64
HP = HA // 2
PAST = 256
CH = TP // P
NEG = -1.0e30
EPS = 1.0e-6
MIN_FORGET = 1.0e-30
WINDOWS = ((128, 1), (512, 4), (2048, 16))
NBUCKET, MAXDIST = 32, 2048

GC = 256
G_IN, G_OUT = 14, 4
NQ = 4
G_UP = G_DOWN = FF // NQ // GC
G_ALL = G_IN + G_OUT + NQ * (G_UP + G_DOWN)
BLK_OUT = 2 * G_IN
BLK_MLP = BLK_OUT + 2 * G_OUT
BLK_Q = 2 * (G_UP + G_DOWN)
B_I, B_F, B_Q, B_V, B_K, B_QA, B_G = 0, 4, 8, 12, 16, 20, 24
MADE = [b + a for b in (B_F, B_Q, B_I, B_V, B_K, B_QA, B_G) for a in range(4)]
G_LV = 6
LEVELS = 8
S_LEVELS = 4
NREL = 640
N_PAR = 4 * KC + HR + HP

BESIDE = {(0, 0): ("rec", 1), (1, 0): ("rec", 2), (2, 0): ("rec", 3), (3, 0): ("rec", 4),
          (3, 1): ("sam", 0, 0), (3, 2): ("sam", 0, 1), (4, 0): ("sam", 0, 2), (4, 1): ("att", 0), (4, 2): ("sam", 0, 3),
          (5, 0): ("sam", 1, 0), (5, 1): ("sam", 1, 1), (5, 2): ("sam", 1, 2), (6, 0): ("sam", 1, 3), (6, 1): ("att", 1),
          (6, 2): ("sam", 2, 0), (7, 0): ("sam", 2, 1), (7, 1): ("sam", 2, 2), (7, 2): ("sam", 2, 3),
          (8, 0): ("sam", 3, 0), (8, 1): ("att", 2), (8, 2): ("sam", 3, 1), (9, 0): ("sam", 3, 2), (9, 1): ("sam", 3, 3),
          (9, 2): ("sam_norm",)}


def rel_buckets(dist):
    exact = NBUCKET // 2
    d = np.maximum(dist, exact).astype(np.float32)
    large = exact + (np.log(d / exact) / np.float32(np.log(MAXDIST / exact)) * (NBUCKET - exact)).astype(np.int32)
    return np.where(dist < exact, dist, np.minimum(large, NBUCKET - 1))


def constants():
    eye = np.eye(P, dtype=np.float32)
    half = np.kron(np.eye(2), np.ones((DH, DH))).astype(np.float32)
    row = np.arange(P)
    head_of_row = ((row % 64) // TB)[:, None] == np.arange(HA)[None]
    tok_of_row = (row // 64 * TB + row % TB)[:, None] == np.arange(2 * TB)[None]
    seq_of_tok = (row // TB)[:, None] == np.arange(NB)[None]
    cst = np.concatenate([eye, half, head_of_row, tok_of_row, seq_of_tok], 1).astype(np.float32)
    s, t = np.arange(P)[:, None], np.arange(P)[None]
    masks = [s == t]
    for lv in range(1, LEVELS):
        h = 1 << (lv - 1)
        masks.append((s // (2 * h) == t // (2 * h)) & (s // h % 2 == 0) & (t // h % 2 == 1))
    masks = np.stack(masks, 1).astype(np.float32)
    dist = 511 - np.arange(NREL)
    count = sum(((dist >= 0) & (dist % d == 0) & (dist <= w)).astype(int) for w, d in WINDOWS)
    rel = np.zeros((NBUCKET + 1, NREL), np.float32)
    rel[rel_buckets(np.maximum(dist, 0)), np.arange(NREL)] = 8.0 * (count > 0)
    rel[NBUCKET] = np.where(count > 0, 8.0 * np.log(np.maximum(count, 1)), NEG)
    return cst, masks, rel


class Steps:

    def __init__(self, eng, sem):
        self.eng, self.sem, self.n = eng, sem, 0

    def __call__(self, ins):
        ins.then_inc(self.sem, 1)
        self.n = self.n + 1

    def wait(self):
        self.eng.wait_ge(self.sem, self.n)

    @contextmanager
    def loop(self, a, b, per):
        start = self.n
        with self.eng.Fori(a, b) as i:
            self.n = start + (i - a) * per
            yield i
        self.n = start + (b - a) * per


def build(nc, xT, w, par, lbr, relb, s0, kcT, vc, cst_d, msk_d, rel_d, yT, sp_o, kT_o, v_o, ss_o, rel_scr):
    ctx = ExitStack()
    at = [16512]

    def place(name, shape, dt=F32, offset=None):
        size = int(np.prod(shape[1:])) * (1 if dt == U8 else 4)
        if offset is None:
            offset = at[0]
            at[0] += (size + 31) // 32 * 32
        return nc.alloc_sbuf_tensor_at(name, list(shape), dt, offset=offset)

    FB = TT * 4
    x = place("x", [P, KC, TT])
    o_hh = at[0]
    hh = place("h_high", [P, KC, TT], F32R)
    o_hl = at[0]
    hl = place("h_rest", [P, KC, TT], F32R)
    raw = [place(f"w_raw{s}", [P, KC, GC]) for s in range(2)]
    whi = [place(f"w_high{s}", [P, KC, GC], F32R) for s in range(2)]
    wlo = [place(f"w_rest{s}", [P, KC, GC], F32R) for s in range(2)]
    t1, o_t2 = place("t1", [P, TT]), at[0]
    t2, t3 = place("t2", [P, TT]), place("t3", [P, TT])
    cst = place("cst", [P, 288])
    ones = place("ones", [P, P])
    masks = place("masks", [P, LEVELS, P], U8)
    ts_cache = place("ts_cache", [P, PAST])
    ts_new = place("ts_new", [P, HP * (TS + 2 * TB)])
    qbig = place("qbig", [P, HP, NB * 64])
    prm = place("prm", [P, N_PAR])
    lb = place("lb", [P, DEPTH, HR])
    lbc = place("lbc", [P, 2, HR])
    eps = place("eps", [P, 1])
    mx = place("mx", [P, 3, 16])
    f_small = [place(f"f_tot{8 << i}", [P, HR, (TT if i == 0 else TP) // (8 << i)]) for i in range(5)]
    o_proj = at[0]
    proj = place("proj", [P, 28, TT])
    o_v = at[0]
    vt = place("v_tok", [P, CH + 1, 512])
    o_kb = at[0]
    kb = place("k_dec", [P, HR, TT])
    assert at[0] <= 229344, at[0]

    ident = cst[:, 0:P]
    half_ones = cst[:, P:2 * P]
    head_mask = cst[:, 256:264]
    tok_sel = cst[:, 264:280]
    seq_mask = cst[:, 280:288]

    va = place("va_tok", [P, CH + 1, 512], offset=o_v)
    g_tmp = [t1, t3]
    states = place("states", [P, HR, CH, P], offset=o_hh)
    f2 = place("f_tot2", [P, HR, TT // 2], offset=o_proj + B_G * FB)
    f4 = place("f_tot4", [P, HR, TT // 4], offset=o_proj + (B_G + 2) * FB)
    kt = place("k_tok", [P, HR, TP], offset=o_hh + 4 * FB)
    kts = place("ks_tok", [P, HR * P], offset=o_t2)
    s_in = [place(f"s_in{s}", [P, NB, P], offset=o_hl + 4096 * s) for s in range(2)]
    sc = place("sc", [P, HR, TP], offset=o_proj + B_I * FB)
    scs = place("scs", [P, HR, TS], offset=o_proj + B_I * FB + 4 * HR * TP)
    v_exp = [place(f"v_exp{s}", [P, NB, P], offset=o_hl + 4 * FB + 4096 * s) for s in range(2)]
    ao = place("ao", [P, HP, TT], offset=o_hl + 4 * FB)
    o_raw = proj[:, B_F:B_F + HR, :]
    q_tmp = proj[:, B_G:B_G + HR, :]
    bias = [place("bias0", [P, HA // 2, TP], offset=o_hh + 4 * FB),
            place("bias1", [P, HA // 2, TP], offset=o_proj + B_F * FB)]
    o_reg = [o_proj + B_Q * FB, o_kb, o_proj + B_V * FB, o_proj + B_I * FB]
    tri = [P * i * (i + 1) // 2 for i in range(CH + 1)]
    prob = [place(f"prob{s}", [P, tri[CH]], offset=o_reg[s]) for s in range(2)]
    pt = [place(f"prob_t{s}", [P, tri[CH]], offset=o_reg[2 + s]) for s in range(2)]
    trj = [tri[CH] - tri[CH - j] for j in range(CH)]
    kc = [place(f"kc{s}", [P, HP, PAST], offset=o_reg[s] + 4 * tri[CH]) for s in range(2)]
    vcs = [place(f"vc{s}", [P, 2, 512], offset=o_reg[2 + s] + 4 * tri[CH]) for s in range(2)]
    ps_s = place("probs_s", [P, PAST + TS], offset=o_proj + B_G * FB)
    pts = place("probs_st", [P, 3 * P], offset=o_proj + (B_G + 1) * FB)
    mo = place("mo", [P, 512], offset=o_proj + (B_G + 2) * FB)
    s_at = {3: (2, 0), 1: (1, 0), 0: (0, 0), 2: (0, P)}
    acc = proj[:, 0:KC, :]
    uh = place("u_high", [P, KC, TT], F32R, offset=o_proj + 8 * FB)
    ul = place("u_rest", [P, KC, TT], F32R, offset=o_proj + 16 * FB)
    ys = proj[:, 8:16, :]
    ssq, root, inv = proj[:, 24, :], proj[:, 25, :], proj[:, 26, :]
    sqs = place("squares", [P, KC, TT], offset=o_v)
    rel_sb = place("rel_sb", [P, HA, NREL], offset=o_proj + 16 * FB)
    rel_r = place("rel_r", [P, NREL], offset=o_proj)
    rel_l = place("rel_l", [P, HA], offset=o_proj + 2 * FB)
    rel_w = place("rel_w", [P, HA, P], offset=o_proj + 4 * FB)
    masks_f = place("masks_f", [P, LEVELS, P], offset=o_proj + 6 * FB)

    ps = ctx.enter_context(nc.psum_tensor("ps", [P, 8, 512], F32))

    def sem(name):
        return ctx.enter_context(nc.semaphore(name))

    c_in, c_tab = sem("c_in"), sem("c_tab")
    c_mm, c_cp, c_set, c_lb, c_exp = sem("c_mm"), sem("c_cp"), sem("c_set"), sem("c_lb"), sem("c_exp")
    c_wide = sem("c_wide")
    with nc.Block() as block:
        @block.sync
        def _(sp):
            for dst, src in ((x[:], xT), (cst[:], cst_d), (masks_f[:], msk_d), (lb[:], lbr),
                             (rel_l[0:NBUCKET, :], relb), (rel_r[0:NBUCKET + 1, :], rel_d)):
                sp.dma_start(dst, src).then_inc(c_in, 16)
            sp.wait_ge(c_cp, 2 * HA)
            sp.dma_start(rel_scr.ap(), rel_sb[:]).then_inc(c_tab, 16)

        @block.gpsimd
        def _(pool):
            for n, (tile, value) in enumerate(((ts_new[:], NEG), (qbig[:], 0.0), (ones[:], 1.0), (eps[:], EPS),
                                               (rel_l[NBUCKET:NBUCKET + 1, :], 1.0))):
                if n:
                    pool.wait_ge(c_set, n)
                nc.gpsimd.memset(tile, value).then_inc(c_set, 1)

        @block.tensor
        def _(pe):
            pe.wait_ge(c_in, 96)
            pe.wait_ge(c_wide, 1)
            for h in range(HA):
                for n, cols in enumerate((slice(0, 512), slice(512, NREL))):
                    if h >= 4:
                        pe.wait_ge(c_cp, 2 * (h - 4) + n + 1)
                    nc.tensor.matmul(ps[:, 2 * (h % 4) + n, 0:cols.stop - cols.start], rel_w[0:NBUCKET + 1, h, :],
                                     rel_r[0:NBUCKET + 1, cols], start=True, stop=True).then_inc(c_mm, 1)

        @block.scalar
        def _(act):
            act.wait_ge(c_lb, 2)
            nc.scalar.activation(lb[:], lb[:], ACT.Exp).then_inc(c_exp, 1)

        @block.vector
        def _(dve):
            own = Steps(dve, c_lb)
            dve.wait_ge(c_in, 96)
            dve.wait_ge(c_set, 5)
            nc.vector.tensor_copy(rel_w[0:NBUCKET + 1], rel_l[0:NBUCKET + 1, :].unsqueeze(2)
                                  .broadcast_to([NBUCKET + 1, HA, P])).then_inc(c_wide, 1)
            own(nc.vector.tensor_tensor(lbc[:, 0, :], lb[:, 0, :], lb[:, 1, :], ALU.max))
            own.wait()
            own(nc.vector.tensor_tensor(lb[:], lb[:], lbc[:, 0:1, :].broadcast_to([P, DEPTH, HR]), ALU.subtract))
            dve.wait_ge(c_exp, 1)
            own(nc.vector.tensor_tensor(lbc[:, 0, :], lb[:, 0, :], lb[:, 1, :], ALU.add))
            own.wait()
            own(nc.vector.reciprocal(lbc[:, 1, :], lbc[:, 0, :]))
            own.wait()
            own(nc.vector.tensor_tensor(lb[:], lb[:], lbc[:, 1:2, :].broadcast_to([P, DEPTH, HR]), ALU.mult))
            own.wait()
            own(nc.vector.tensor_tensor(lbc[:, 0, :], lb[:, 0, :], lb[:, 1, :], ALU.add))
            own.wait()
            own(nc.vector.tensor_tensor(lb[:, 1, :], lbc[:, 0, :], lb[:, 0, :], ALU.subtract))
            own.wait()
            own(nc.vector.memset(lb[:, 0, :], 0.0))
            own(nc.vector.tensor_copy(masks[:], masks_f[:]))
            for h in range(HA):
                for n, cols in enumerate((slice(0, 512), slice(512, NREL))):
                    dve.wait_ge(c_mm, 2 * h + n + 1)
                    nc.vector.tensor_copy(rel_sb[:, h, cols], ps[:, 2 * (h % 4) + n, 0:cols.stop - cols.start])\
                        .then_inc(c_cp, 1)
            own.wait()
            dve.wait_ge(c_cp, 2 * HA)

    lay = ["w_in0", "w_in1", "w_hi", "w_ready", "blk", "free", "prm_in",
           "sq", "ssq", "ms", "root", "inv", "scaled", "h_hi", "h_even", "h_odd", "xr", "xr_odd", "dv",
           "e_f", "e_q", "e_g",
           "v_t", "v_there", "lv", "sc_set", "scs_set", "q_up", "k_up",
           "k_t", "k_there", "u_done", "st_done", "o_done", "o_there", "os_set",
           "s0_in0", "s0_in1", "s_out0", "s_out1", "v_wide", "su_done", "s_new",
           "r_sq", "r_ms", "r_root", "r_scaled", "r_hi", "r_lo",
           "va_t", "va_there", "b_in0", "b_in1", "qb", "s_done", "s_max", "p_exp", "p_norm", "p_t", "pt_there",
           "pv_done", "ao_there",
           "kc_in0", "kc_in1", "vc_in0", "vc_in1", "ss_done", "ss_max", "sp_exp", "sp_norm", "sp_t", "spt_there",
           "spv_done", "mo_set", "sel_done",
           "a_sq", "a_ms", "a_root", "a_scaled", "a_hi", "a_lo", "u_set",
           "g_gated", "so_there", "n_sq", "n_ms", "n_root", "n_scaled", "n_hi", "ts_in", "st_out", "k_out", "v_out0", "v_out1"]
    S = {n: sem(n) for n in lay}
    nums = [S[n].num for n in lay]
    assert nums == list(range(nums[0], nums[0] + len(nums)))

    def pair_of(m, part=slice(0, P)):
        return ps[part, 2 * m:2 * m + 2, 0:HT]

    def halves(ap):
        return ap.rearrange("p (a t) -> p a t", a=2)

    with nc.Fori(0, DEPTH) as l:
        with nc.Block() as block:
            @block.sync
            def _(sp):
                def load(g, s):
                    sp.dma_start(raw[s][:].rearrange("p a b -> p (a b)"),
                                 w[bass.ds(l * G_ALL + g, 1)].rearrange("o p n -> p (o n)")).then_inc(S[f"w_in{s}"], 16)

                load(0, 0)
                load(1, 1)
                with sp.Fori(1, G_ALL // 2) as i:
                    for s in range(2):
                        sp.wait_ge(S["w_ready"], 2 * i + s - 1)
                        load(2 * i + s, s)

            @block.gpsimd
            def _(pool):

                def rest(a, b):
                    with pool.Fori(a, b) as i:
                        for s in range(2):
                            pool.wait_ge(S["w_hi"], 2 * i + s + 1)
                            nc.gpsimd.tensor_tensor(wlo[s][:], raw[s][:], whi[s][:].bitcast(F32),
                                                    ALU.subtract).then_inc(S["w_ready"], 1)

                def rest_of(g, s):
                    pool.wait_ge(S["w_hi"], g + 1)
                    nc.gpsimd.tensor_tensor(wlo[s][:], raw[s][:], whi[s][:].bitcast(F32),
                                            ALU.subtract).then_inc(S["w_ready"], 1)

                def update_odd(k):
                    for c in range(1, KC, 2):
                        pool.wait_ge(S["scaled"], KC * k + c + 1)
                        nc.gpsimd.tensor_tensor(x[:, c, :], x[:, c, :], ys[:, c, :], ALU.add).then_inc(S["xr_odd"], 1)

                def rest_odd(k):
                    for c in range(1, KC, 2):
                        pool.wait_ge(S["h_hi"], KC * (k // 2) + c + 1)
                        nc.gpsimd.tensor_tensor(hl[:, c, :], ys[:, c, :], hh[:, c, :].bitcast(F32),
                                                ALU.subtract).then_inc(S["h_odd"], 1)

                rest(0, 1)
                rest_odd(0)
                rest(1, G_LV // 2 + 1)
                rest_of(G_LV + 2, 0)

                tot = [proj[:, B_F:B_F + HR, :], f2[:], f4[:]] + [f[:] for f in f_small]
                for lv in range(1, LEVELS):
                    rest_of(G_LV + 2 + lv, lv % 2)
                    h = 1 << (lv - 1)
                    wd = TT if h <= 4 else TP
                    for a in range(HR):
                        pool.wait_ge(S["lv"], HR * lv + a + 1)
                        if lv > 1:
                            pool.wait_ge(S["k_up"], 2 * (HR * lv + a + 1))
                        f = tot[lv - 1][:, a, 0:wd // h].rearrange("p (n two) -> p n two", two=2)
                        keys = kb[:, a, 0:wd].rearrange("p (n two h) -> p n two h", two=2, h=h)
                        n = wd // (2 * h)
                        nc.gpsimd.tensor_tensor(keys[:, :, 0, :], keys[:, :, 0, :],
                                                f[:, :, 1].unsqueeze(2).broadcast_to([P, n, h]),
                                                ALU.mult).then_inc(S["k_up"], 1)
                        nc.gpsimd.tensor_tensor(tot[lv][:, a, 0:n], f[:, :, 0], f[:, :, 1], ALU.mult).then_inc(S["k_up"], 1)

                pool.wait_ge(S["lv"], HR * LEVELS)
                for a in range(HR):
                    if a >= 2:
                        pool.wait_ge(S["su_done"], a - 1)
                    nc.gpsimd.tensor_tensor(v_exp[a % 2][0:TS],
                                            vt[0:TS, CH, a * P:a * P + P].unsqueeze(1).broadcast_to([TS, NB, P]),
                                            seq_mask[0:TS].unsqueeze(2).broadcast_to([TS, NB, P]),
                                            ALU.mult).then_inc(S["v_wide"], 1)

                rest(G_IN // 2 + 1, (G_IN + G_OUT) // 2 + 1)
                update_odd(1)
                rest_odd(2)
                rest((G_IN + G_OUT) // 2 + 1, G_ALL // 2)
                update_odd(3)

            @block.scalar
            def _(act):

                def high(g, s, first=False):
                    act.wait_ge(S[f"w_in{s}"], 8 * (g - s) + 16)
                    if not first:
                        act.wait_ge(S["blk"], 2 * g - 2)
                    nc.scalar.activation(whi[s][:], raw[s][:], ACT.Copy).then_inc(S["w_hi"], 1)

                def square(k, src, c):
                    nc.scalar.activation(sqs[:, c, :], src[:, c, :], ACT.Square).then_inc(S["sq"], 1)

                def norm_root(k):
                    act.wait_ge(S["ms"], k + 1)
                    nc.scalar.activation(halves(root), ps[:, 4:6, 0:HT], ACT.Sqrt, bias=eps[:],
                                         scale=1.0 / D).then_inc(S["root"], 1)

                def h_high(k):
                    for c in range(KC):
                        act.wait_ge(S["scaled"], KC * k + c + 1)
                        nc.scalar.activation(hh[:, c, :], ys[:, c, :], ACT.Copy).then_inc(S["h_hi"], 1)

                act.dma_start(prm[:], par[bass.ds(l, 1)].rearrange("o p n -> p (o n)")).then_inc(S["prm_in"], 16)
                high(0, 0, True)
                high(1, 1, True)
                for c in range(KC):
                    square(0, x, c)
                norm_root(0)
                h_high(0)

                act.wait_ge(c_tab, 16)
                for b in range(2):
                    for h in range(HA):
                        rows = slice(64 * b + TB * h, 64 * b + TB * h + TB)
                        act.dma_start(ts_cache[rows, :], bass.AP(rel_scr, h * NREL + 255, [[HA * NREL - 1, TB], [1, PAST]]))\
                            .then_inc(S["ts_in"], 16)
                        own_keys = ts_new[rows, :].rearrange("p (pair n) -> p pair n", pair=HP)[:, :, TB * b:TB * b + TB]
                        act.dma_start(own_keys, bass.AP(rel_scr, h * NREL + 511, [[HA * NREL - 1, TB], [0, HP], [1, TB]]))\
                            .then_inc(S["ts_in"], 16)

                for b in range(BLK_OUT):
                    if b % 2:
                        high(b // 2 + 2, b // 2 % 2)
                    made = MADE[b]
                    if B_F <= made < B_F + HR:
                        act.wait_ge(S["free"], 2 + b + 1)
                        nc.scalar.activation(kb[:, made - B_F, :], proj[:, made, :], ACT.Exp, scale=-1.0).then_inc(S["e_f"], 1)
                    elif B_Q <= made < B_Q + HR:
                        act.wait_ge(S["free"], 2 + b + 1)
                        nc.scalar.activation(q_tmp[:, made - B_Q, :], proj[:, made, :], ACT.Exp, scale=-1.0).then_inc(S["e_q"], 1)
                    elif B_G <= made < B_G + HR:
                        a = made - B_G
                        act.wait_ge(S["free"], 2 + b + 1)
                        if a >= 2:
                            act.wait_ge(S["g_gated"], a - 1)
                        nc.scalar.activation(g_tmp[a % 2][:], proj[:, made, :], ACT.Exp, scale=-1.0).then_inc(S["e_g"], 1)
                    elif made == B_I + HR - 1:
                        for t in range(CH + 1):
                            rows = P if t < CH else TS
                            act.wait_ge(S["v_t"], t + 1)
                            nc.scalar.activation(vt[0:rows, t, :], ps[0:rows, 4 + t % 4, :], ACT.Copy).then_inc(S["v_there"], 1)
                act.wait_ge(S["free"], 2 + BLK_OUT)
                act.dma_start(kT_o[bass.ds(l, 1)].rearrange("o p j t -> p (o j) t"),
                              proj[:, B_K:B_K + HP, :]).then_inc(S["k_out"], 16)

                def load_state(a):
                    act.dma_start(s_in[a % 2][:], s0[bass.ds(l * HR + a, 1)].rearrange("o p b v -> p (o b) v"))\
                        .then_inc(S[f"s0_in{a % 2}"], 16)

                load_state(0)
                load_state(1)
                for a in range(HR):
                    act.wait_ge(S["k_t"], a + 1)
                    nc.scalar.activation(kt[:, a, :], ps[:, 4 + a, :], ACT.Copy).then_inc(S["k_there"], 1)
                act.wait_ge(S["k_t"], HR + 1)
                nc.scalar.activation(kts[0:TS, :], ps[0:TS, 0, :], ACT.Copy).then_inc(S["k_there"], 1)
                act.wait_ge(S["u_done"], HR)
                act.dma_start(bias[0][:], bass.AP(rel_scr, 127, [[HA * NREL - 1, P], [NREL, HP], [1, TP]])).then_inc(S["b_in0"], 16)
                act.wait_ge(S["st_done"], HR)
                act.dma_start(sp_o[bass.ds(l, 1)].rearrange("o p h v -> p (o h) v"),
                              states[:, :, CH - 1, :]).then_inc(S["st_out"], 16)
                for a in range(HR):
                    act.wait_ge(S["o_done"], a + 1)
                    nc.scalar.activation(o_raw[:, a, 0:TP], ps[:, 4 + a, :], ACT.Copy).then_inc(S["o_there"], 1)
                for a in range(HR):
                    act.wait_ge(S["s_new"], a + 1)
                    act.dma_start(ss_o[bass.ds(l * HR + a, 1)].rearrange("o p b v -> p (o b) v"),
                                  s_in[a % 2][:]).then_inc(S[f"s_out{a % 2}"], 16)
                    if a + 2 < HR:
                        act.wait_ge(S[f"s_out{a % 2}"], 16)
                        load_state(a + 2)
                nc.scalar.activation(o_raw[:, :, TP:TT], ps[:, 0, 0:HR * TS].rearrange("p (a t) -> p a t", a=HR),
                                     ACT.Copy).then_inc(S["o_there"], 1)
                act.wait_ge(S["os_set"], 1)

                def rec(a):
                    if a:
                        act.wait_ge(S["r_scaled"], a)
                        if a == 1:
                            act.wait_ge(S["st_out"], 16)
                        nc.scalar.activation(hh[:, a - 1, :], t3[:], ACT.Copy).then_inc(S["r_hi"], 1)
                    if a < HR:
                        act.wait_ge(S["r_ms"], a + 1)
                        nc.scalar.activation(halves(t2[:]), ps[:, 6:8, 0:HT], ACT.Sqrt, bias=eps[:],
                                             scale=1.0 / P).then_inc(S["r_root"], 1)
                    if a < HR - 1:
                        nc.scalar.activation(t1[:], o_raw[:, a + 1, :], ACT.Square).then_inc(S["r_sq"], 1)
                    if a == HR:
                        act.dma_start(bias[1][:], bass.AP(rel_scr, HP * NREL + 127, [[HA * NREL - 1, P], [NREL, HP], [1, TP]]))\
                            .then_inc(S["b_in1"], 16)

                def att(a):
                    if 0 < a < HP - 1:
                        act.wait_ge(S["a_scaled"], a)
                        nc.scalar.activation(hh[:, HR + a - 1, 0:TP], t3[:, 0:TP], ACT.Copy).then_inc(S["a_hi"], 1)
                    act.wait_ge(S["a_ms"], a + 1)
                    nc.scalar.activation(t2[:, 0:TP], ps[:, 7, :], ACT.Sqrt, bias=eps[:], scale=1.0 / DH).then_inc(S["a_root"], 1)

                def sam_norm():
                    act.wait_ge(S["a_scaled"], HP - 1)
                    nc.scalar.activation(hh[:, HR + HP - 2, 0:TP], t3[:, 0:TP], ACT.Copy).then_inc(S["a_hi"], 1)
                    act.wait_ge(S["so_there"], HP)
                    nc.scalar.activation(t1[:, 0:HP * TS].rearrange("p (a t) -> p a t", a=HP), ao[:, :, TP:TT],
                                         ACT.Square).then_inc(S["n_sq"], 1)
                    act.wait_ge(S["n_ms"], 1)
                    nc.scalar.activation(t2[:, 0:HP * TS], ps[:, 7, 0:HP * TS], ACT.Sqrt, bias=eps[:],
                                         scale=1.0 / DH).then_inc(S["n_root"], 1)

                def square_pair(a):
                    if a:
                        act.wait_ge(S["a_ms"], a)
                    nc.scalar.activation(t1[:, 0:TP], ao[:, a, 0:TP], ACT.Square).then_inc(S["a_sq"], 1)

                def sam(p2, k):
                    if k == 0:
                        act.wait_ge(S["ss_max"], 4 * (p2 + 1))
                        nc.scalar.activation(ps_s[:], ps_s[:], ACT.Exp, bias=mx[:, 2, 1:2], scale=0.125,
                                             accum_out=mx[:, 2, 2:3]).then_inc(S["sp_exp"], 1)
                        if p2 + 1 < HP:
                            load_k(2 * p2 + 2)
                            load_k(2 * p2 + 3)
                    if k == 1:
                        act.wait_ge(S["sp_t"], p2 + 1)
                        nc.scalar.activation(pts[:, 0:2 * P], ps[:, 7, 0:2 * P], ACT.Copy).then_inc(S["spt_there"], 1)
                        nc.scalar.activation(pts[0:TS, 2 * P:3 * P], ps[0:TS, 7, 2 * P:3 * P], ACT.Copy).then_inc(S["spt_there"], 1)
                    if k == 3:
                        act.wait_ge(S["sel_done"], p2 + 1)
                        nc.scalar.activation(ao[:, :, TP + 2 * TB * p2:TP + 2 * TB * (p2 + 1)],
                                             ps[:, 7, 0:HP * 2 * TB].rearrange("p (a t) -> p a t", a=HP),
                                             ACT.Copy).then_inc(S["so_there"], 1)
                        if p2 + 1 < HP:
                            load_v(2 * p2 + 2)
                            load_v(2 * p2 + 3)

                steps = {"rec": rec, "att": att, "sam": sam, "sam_norm": sam_norm}

                def beside(h, place_):
                    if (h, place_) in BESIDE:
                        name, *which = BESIDE[h, place_]
                        steps[name](*which)

                def load_k(b):
                    s = b % 2
                    act.dma_start(kc[s][:], kcT[bass.ds(l * NB + b, 1)].rearrange("o p j n -> p (o j) n")).then_inc(S[f"kc_in{s}"], 16)

                def load_v(b):
                    s = b % 2
                    act.dma_start(vcs[s][:], vc[bass.ds(l * NB + b, 1)].rearrange("o p j n -> p (o j) n")).then_inc(S[f"vc_in{s}"], 16)

                nc.scalar.activation(t1[:], o_raw[:, 0, :], ACT.Square).then_inc(S["r_sq"], 1)
                for t in range(CH + 1):
                    rows = P if t < CH else TS
                    act.wait_ge(S["va_t"], t + 1)
                    nc.scalar.activation(va[0:rows, t, :], ps[0:rows, t % 4, :], ACT.Copy).then_inc(S["va_there"], 1)
                rec(0)
                act.wait_ge(S["va_there"], CH + 1)
                act.dma_start(v_o[bass.ds(l, 1), 0:TP, :].rearrange("o (t p) n -> p (o t) n", p=P),
                              va[:, 0:CH, :]).then_inc(S["v_out0"], 16)
                act.dma_start(v_o[bass.ds(l, 1), TP:TT, :].rearrange("o p n -> p (o n)"),
                              va[0:TS, CH, :]).then_inc(S["v_out1"], 16)
                for b in range(2):
                    load_k(b)
                    load_v(b)
                for h in range(HA + 2):
                    if h < HA:
                        pr, m = prob[h % 2], mx[:, h % 2, :]
                        act.wait_ge(S["s_max"], (CH + 1) * (h + 1))
                        for i in range(CH):
                            nc.scalar.activation(pr[:, tri[i]:tri[i + 1]], pr[:, tri[i]:tri[i + 1]], ACT.Exp,
                                                 bias=m[:, 4 + i:5 + i], scale=0.125,
                                                 accum_out=m[:, 8 + i:9 + i]).then_inc(S["p_exp"], 1)
                    beside(h, 0)
                    if 0 < h <= HA:
                        g = h - 1
                        if g >= 2:
                            act.wait_ge(S["pv_done"], g - 1)
                        for n, (bank, j0, j1) in enumerate(((3, 0, 1), (4, 1, 2), (5, 2, 4))):
                            act.wait_ge(S["p_t"], 3 * g + n + 1)
                            width = (trj + [tri[CH]])[j1] - trj[j0]
                            nc.scalar.activation(pt[g % 2][:, trj[j0]:trj[j0] + width], ps[:, bank, 0:width],
                                                 ACT.Copy).then_inc(S["pt_there"], 1)
                    beside(h, 1)
                    if h > 1 and h % 2:
                        act.wait_ge(S["pv_done"], h - 1)
                        nc.scalar.activation(ao[:, (h - 3) // 2, 0:TP], ps[:, 6, :], ACT.Copy).then_inc(S["ao_there"], 1)
                        if h < HA + 1:
                            act.wait_ge(S["ao_there"], (h - 1) // 2)
                            square_pair((h - 3) // 2)
                    beside(h, 2)
                act.wait_ge(S["ao_there"], HP)
                square_pair(HP - 1)
                act.wait_ge(S["n_scaled"], 1)
                nc.scalar.activation(hh[:, HR:HR + HP, TP:TT], t3[:, 0:HP * TS].rearrange("p (a t) -> p a t", a=HP),
                                     ACT.Copy).then_inc(S["n_hi"], 1)
                att(HP - 1)
                act.wait_ge(S["a_scaled"], HP)
                nc.scalar.activation(hh[:, HR + HP - 1, 0:TP], t3[:, 0:TP], ACT.Copy).then_inc(S["a_hi"], 1)

                act.wait_ge(S["k_out"], 16)
                act.wait_ge(S["v_out0"], 16)
                act.wait_ge(S["v_out1"], 16)
                for g in range(G_OUT):
                    high(G_IN + 2 + g, g % 2)
                    for c in range(2 * g, 2 * g + 2):
                        act.wait_ge(S["free"], 2 + BLK_OUT + c + 1)
                        square(1, acc, c)
                norm_root(1)
                for c in range(KC):
                    act.wait_ge(S["xr_odd" if c % 2 else "xr"], c // 2 + 1)
                    square(2, x, c)
                norm_root(2)
                h_high(2)
                with act.Fori((G_IN + G_OUT) // 2 + 1, G_ALL // 2 - 1) as i:
                    for s in range(2):
                        high(2 * i + s, s)
                high(G_ALL - 2, 0)
                for c in range(KC):
                    if c == 2:
                        high(G_ALL - 1, 1)
                    act.wait_ge(S["free"], 2 + 2 * (G_ALL - G_DOWN) + c + 1)
                    square(3, acc, c)
                norm_root(3)
                for out, n in (("st_out", 16), ("v_out0", 16), ("v_out1", 16), ("s_out0", 32), ("s_out1", 32)):
                    act.wait_ge(S[out], n)

            @block.tensor
            def _(pe):
                def group(g, s, src_hi=hh, src_lo=hl, ready=None):
                    pe.wait_ge(S["w_ready"], g + 1)
                    for m in range(2):
                        cols = slice(m * P, m * P + P)
                        pe.wait_ge(S["free"], 2 * g + (m + 1))
                        for c in range(KC):
                            if ready and s == 0 and m == 0:
                                name, value = ready(c)
                                pe.wait_ge(S[name], value)
                            for n, (wt, act_) in enumerate(((wlo, src_hi), (whi, src_lo), (whi, src_hi))):
                                for half in range(2):
                                    last = pe.matmul(ps[:, 2 * m + half, 0:HT], wt[s][:, c, cols],
                                                     act_[:, c, half * HT:half * HT + HT],
                                                     start=(c == 0 and n == 0), stop=(c == KC - 1 and n == 2))
                        last.then_inc(S["blk"], 1)

                def gemm(first_group, groups, src_hi, src_lo, ready):
                    with pe.Fori(0, groups // 2) as i:
                        for s in range(2):
                            group(2 * i + (first_group + s), s, src_hi, src_lo, ready)

                def norm_sum(k):
                    blocks = [sqs[:, c, :] for c in range(KC)] if k % 2 == 0 else [ssq, sqs[:, KC - 1, :]]
                    for n, blk in enumerate(blocks):
                        if k % 2 and n == 0:
                            pe.wait_ge(S["ssq"], (KC - 2) * (k // 2 + 1))
                        else:
                            pe.wait_ge(S["sq"], KC * k + (KC if k % 2 else n + 1))
                        for half in range(2):
                            last = pe.matmul(ps[:, 4 + half, 0:HT], ones[:], blk[:, half * HT:half * HT + HT],
                                             start=(n == 0), stop=(n == len(blocks) - 1))
                    last.then_inc(S["ms"], 1)

                def normed(k):
                    return lambda c: ("h_odd" if c % 2 else "h_even", KC // 2 * (k // 2) + c // 2 + 1)

                norm_sum(0)
                def level(lv, sampled):
                    for a in range(HR):
                        bank = 4 + a % 3
                        pe.wait_ge(S["q_up"], HR * lv + (a + 1))
                        pe.wait_ge(S["k_up"], 2 * HR * lv + (2 * a + 2))
                        if a == HR - 1:
                            pe.wait_ge(S["sc_set"], HR * lv + (1 + HR))
                        else:
                            pe.wait_ge(S["sc_set"], HR * lv + HR)
                        for c in range(CH):
                            last = pe.matmul(ps[:, bank, c * P:c * P + P], kb[:, a, c * P:c * P + P],
                                             proj[:, B_Q + a, c * P:c * P + P], start=True, stop=True)
                        if sampled:
                            if a == 0:
                                pe.wait_ge(S["scs_set"], lv + 1)
                            last = pe.matmul(ps[0:TS, 7, a * TS:a * TS + TS], kb[:, a, TP:TT],
                                             proj[:, B_Q + a, TP:TT], start=True, stop=True)
                        last.then_inc(S["lv"], 1)

                gemm(0, G_LV, hh, hl, normed(0))
                pe.wait_ge(S["free"], 2 + 2 * G_LV)
                for t in range(CH + 1):
                    cols = P if t < CH else TS
                    if t == CH:
                        pe.wait_ge(S["v_there"], 1)
                    for c in range(HR):
                        last = pe.transpose(ps[0:cols, 4 + t % 4, c * P:c * P + P], proj[:, B_I + c, t * P:t * P + cols], ident)
                    last.then_inc(S["v_t"], 1)
                for first, last_lv in ((0, S_LEVELS), (S_LEVELS, LEVELS)):
                    with pe.Fori(first // 2, last_lv // 2) as i:
                        pe.wait_ge(S["v_there"], CH + 1)
                        for s in range(2):
                            group(2 * i + (G_LV + s), s)
                            level(2 * i + s, last_lv == S_LEVELS)
                pe.wait_ge(S["scs_set"], S_LEVELS + 1)
                for a in range(HR):
                    pe.wait_ge(S["k_up"], 2 * (HR * LEVELS + a + 1))
                    pe.wait_ge(S["sc_set"], HR * LEVELS + HR)
                    for c in range(CH):
                        last = pe.transpose(ps[:, 4 + a, c * P:c * P + P], kb[:, a, c * P:c * P + P], ident)
                    last.then_inc(S["k_t"], 1)
                for a in range(HR):
                    last = pe.transpose(ps[0:TS, 0, a * P:a * P + P], kb[:, a, TP:TT], ident)
                last.then_inc(S["k_t"], 1)
                for a in range(HR):
                    pe.wait_ge(S["k_there"], (a + 1) if a < 3 else HR + 1)
                    for c in range(CH):
                        last = pe.matmul(ps[:, (a + 1) % 4, c * P:c * P + P], kt[:, a, c * P:c * P + P],
                                         vt[:, c, a * P:a * P + P], start=True, stop=True)
                    last.then_inc(S["u_done"], 1)
                for a in range(HR):
                    pe.wait_ge(S["st_done"], a + 1)
                    pe.wait_ge(S["q_up"], HR * LEVELS + a + 1)
                    for c in range(CH):
                        cs = slice(c * P, c * P + P)
                        last = pe.matmul(ps[:, 4 + a, cs], vt[:, c, a * P:a * P + P], sc[:, a, cs], start=True, stop=(c == 0))
                        if c:
                            last = pe.matmul(ps[:, 4 + a, cs], states[:, a, c - 1, :], proj[:, B_Q + a, cs], start=False, stop=True)
                    last.then_inc(S["o_done"], 1)
                for a in range(HR):
                    pe.wait_ge(S[f"s0_in{a % 2}"], 16 * (a // 2 + 1))
                    pe.matmul(ps[:, 0, a * TS:a * TS + TS], vt[0:TS, CH, a * P:a * P + P], scs[0:TS, a, :],
                              start=True, stop=True)
                    for b in range(NB):
                        o0 = a * TS + b * TB
                        pe.matmul(ps[:, 1, o0:o0 + TB], s_in[a % 2][:, b, :],
                                  proj[:, B_Q + a, TP + b * TB:TP + b * TB + TB], start=True, stop=True)
                    pe.wait_ge(S["v_wide"], a + 1)
                    if a:
                        pe.wait_ge(S["s_new"], a)
                    for half in range(2):
                        last = pe.matmul(ps[:, 2 + half, :], kts[0:TS, a * P:a * P + P],
                                         v_exp[a % 2][0:TS, 4 * half:4 * half + 4, :], start=True, stop=True)
                    last.then_inc(S["su_done"], 1)
                pe.wait_ge(S["os_set"], 1)
                for t in range(CH + 1):
                    cols = P if t < CH else TS
                    if t == CH:
                        pe.wait_ge(S["va_there"], 1)
                    for c in range(HP):
                        last = pe.transpose(ps[0:cols, t % 4, c * P:c * P + P], proj[:, B_V + c, t * P:t * P + cols], ident)
                    last.then_inc(S["va_t"], 1)

                def rec(a):
                    if a < HR:
                        pe.wait_ge(S["r_sq"], a + 1)
                        for half in range(2):
                            last = pe.matmul(ps[:, 6 + half, 0:HT], ones[:], t1[:, half * HT:half * HT + HT],
                                             start=True, stop=True)
                        last.then_inc(S["r_ms"], 1)

                def att(a):
                    pe.wait_ge(S["a_sq"], a + 1)
                    free_7()
                    pe.matmul(ps[:, 7, :], half_ones, t1[:, 0:TP], start=True, stop=True).then_inc(S["a_ms"], 1)
                    bank_7[0] = ("a_root", a + 1)

                def sam_norm():
                    pe.wait_ge(S["n_sq"], 1)
                    free_7()
                    pe.matmul(ps[:, 7, 0:HP * TS], half_ones, t1[:, 0:HP * TS], start=True, stop=True).then_inc(S["n_ms"], 1)
                    bank_7[0] = ("n_root", 1)

                def sam(p2, k):
                    free_7()
                    if k == 0:
                        for s in range(2):
                            pe.wait_ge(S[f"kc_in{s}"], 16 * (p2 + 1))
                            r = slice(64 * s, 64 * s + 64)
                            for j in range(HP):
                                q0 = (2 * p2 + s) * 64
                                pe.matmul(ps[r, 7, 0:PAST], qbig[:, j, q0:q0 + 64], kc[s][:, j, :],
                                          start=(j == 0), stop=(j == HP - 1))
                        for j in range(HP):
                            last = pe.matmul(ps[:, 7, PAST:PAST + TS], qbig[:, j, p2 * P:p2 * P + P], proj[:, B_K + j, TP:TT],
                                             start=(j == 0), stop=(j == HP - 1))
                        last.then_inc(S["ss_done"], 1)
                        bank_7[0] = ("ss_max", 4 * p2 + 2)
                    if k == 1:
                        pe.wait_ge(S["sp_norm"], p2 + 1)
                        for k2 in range(2):
                            pe.transpose(ps[:, 7, k2 * P:k2 * P + P], ps_s[:, k2 * P:k2 * P + P], ident)
                        pe.transpose(ps[0:TS, 7, 2 * P:3 * P], ps_s[:, PAST:PAST + TS], ident).then_inc(S["sp_t"], 1)
                        bank_7[0] = ("spt_there", 2 * (p2 + 1))
                    if k == 2:
                        for s in range(2):
                            pe.wait_ge(S[f"vc_in{s}"], 16 * (p2 + 1))
                            for k2 in range(2):
                                pe.matmul(ps[64 * s:64 * s + 64, 7, :], pts[:, k2 * P + 64 * s:k2 * P + 64 * s + 64],
                                          vcs[s][:, k2, :], start=(k2 == 0), stop=False)
                        last = pe.matmul(ps[:, 7, :], pts[0:TS, 2 * P:3 * P], va[0:TS, CH, :], start=False, stop=True)
                        last.then_inc(S["spv_done"], 1)
                        bank_7[0] = ("mo_set", p2 + 1)
                    if k == 3:
                        for c in range(HP):
                            last = pe.matmul(ps[:, 7, c * 2 * TB:(c + 1) * 2 * TB], mo[:, c * P:c * P + P], tok_sel,
                                             start=True, stop=True)
                        last.then_inc(S["sel_done"], 1)
                        bank_7[0] = ("so_there", p2 + 1)

                steps = {"rec": rec, "att": att, "sam": sam, "sam_norm": sam_norm}

                def beside(h, place_):
                    if (h, place_) in BESIDE:
                        name, *which = BESIDE[h, place_]
                        steps[name](*which)

                bank_7 = [("r_root", HR)]

                def free_7():
                    pe.wait_ge(S[bank_7[0][0]], bank_7[0][1])

                pe.wait_ge(S["qb"], 1)
                rec(0)
                for h in range(HA + 2):
                    if h < HA:
                        r = slice(DH * (h % 2), DH * (h % 2) + DH)
                        if h:
                            pe.wait_ge(S["s_max"], (CH + 1) * h)
                        else:
                            pe.wait_ge(S["va_there"], CH + 1)
                        for i, (bank, c0) in s_at.items():
                            last = pe.matmul(ps[:, bank, c0:c0 + (i + 1) * P], proj[r, B_QA + h // 2, i * P:i * P + P],
                                             proj[r, B_K + h // 2, 0:(i + 1) * P], start=True, stop=True)
                            if i:
                                last.then_inc(S["s_done"], 1)
                    beside(h, 0)
                    if 0 < h <= HA:
                        g = h - 1
                        pe.wait_ge(S["p_norm"], CH * (g + 1))
                        if g:
                            pe.wait_ge(S["pt_there"], 3 * g)
                        for bank, js in ((3, (0,)), (4, (1,)), (5, (2, 3))):
                            for j in js:
                                for i in range(j, CH):
                                    c0 = trj[j] - trj[js[0]] + (i - j) * P
                                    last = pe.transpose(ps[:, bank, c0:c0 + P],
                                                        prob[g % 2][:, tri[i] + j * P:tri[i] + j * P + P], ident)
                            last.then_inc(S["p_t"], 1)
                    beside(h, 1)
                    if h > 1:
                        g = h - 2
                        r = slice(DH * (g % 2), DH * (g % 2) + DH)
                        pe.wait_ge(S["pt_there"], 3 * (g + 1))
                        if g == 0:
                            pe.wait_ge(S["r_root"], HR)
                        elif g % 2 == 0:
                            pe.wait_ge(S["ao_there"], g // 2)
                        for i in range(CH):
                            for j in range(i + 1):
                                c0 = trj[j] + (i - j) * P
                                last = pe.matmul(ps[r, 6, i * P:i * P + P], va[:, j, g * DH:g * DH + DH],
                                                 pt[g % 2][:, c0:c0 + P], start=(j == 0), stop=(j == i))
                        last.then_inc(S["pv_done"], 1)
                    beside(h, 2)
                att(HP - 1)

                gemm(G_IN, G_OUT, hh, hl, lambda c: ("r_lo", c + 1) if c < HR else ("a_lo", HP if c < KC - 1 else HP + 1))
                norm_sum(1)
                norm_sum(2)
                with pe.Fori(0, NQ) as q:
                    g0 = q * (G_UP + G_DOWN) + (G_IN + G_OUT)
                    gemm(g0, G_UP, hh, hl, normed(2))
                    gemm(g0 + G_UP, G_DOWN, uh, ul, lambda c: ("u_set", q * KC + (c + 1)))
                norm_sum(3)

            @block.vector
            def _(dve):
                own = Steps(dve, S["dv"])
                V = nc.vector

                def sum_squares(k, c):
                    if c < 2:
                        return
                    n = (KC - 2) * (k // 2)
                    dve.wait_ge(S["sq"], KC * k + c)
                    if c > 2:
                        dve.wait_ge(S["ssq"], n + c - 2)
                    V.tensor_tensor(ssq, sqs[:, 0, :] if c == 2 else ssq, sqs[:, c - 1, :], ALU.add).then_inc(S["ssq"], 1)

                def norm_apply(k, gains, post):
                    dve.wait_ge(S["root"], k + 1)
                    V.reciprocal(inv, root).then_inc(S["inv"], 1)
                    dve.wait_ge(S["inv"], k + 1)
                    src = acc if post else x
                    for c in range(KC + 2):
                        if c < KC:
                            V.scalar_tensor_tensor(ys[:, c, :], src[:, c, :], gains[:, c:c + 1], inv,
                                                   ALU.mult, ALU.mult).then_inc(S["scaled"], 1)
                        b = c - 1 if post else c - 2
                        if b < 0 or b % 2 or b >= KC:
                            continue
                        if post:
                            dve.wait_ge(S["scaled"], KC * k + b + 1)
                            V.tensor_tensor(x[:, b, :], x[:, b, :], ys[:, b, :], ALU.add).then_inc(S["xr"], 1)
                        else:
                            dve.wait_ge(S["h_hi"], KC * (k // 2) + b + 1)
                            V.tensor_tensor(hl[:, b, :], ys[:, b, :], hh[:, b, :].bitcast(F32),
                                            ALU.subtract).then_inc(S["h_even"], 1)

                def sigmoid_parts(e):
                    own(V.tensor_scalar(e, e, 1.0, None, ALU.add))
                    own.wait()
                    own(V.reciprocal(e, e))
                    own.wait()

                V.memset(mx[:], 0.0).then_inc(S["free"], 2)
                own(V.tensor_copy(lbc[:, 0:1, :], lb[:, bass.ds(l, 1), :]))
                own.wait()
                own(V.tensor_scalar(lbc[:, 1, :], lbc[:, 0, :], -1.0, 1.0, ALU.mult, ALU.add))
                dve.wait_ge(S["prm_in"], 16)
                norm_apply(0, prm[:, 0:KC], False)

                dve.wait_ge(c_tab, 16)
                zf, qq, gg = (proj[:, b0:b0 + HR, :] for b0 in (B_F, B_Q, B_G))
                def gate_f(a):
                    k, f = kb[:, a, :], zf[:, a, :]
                    dve.wait_ge(S["e_f"], a + 1)
                    own(V.tensor_scalar(f, k, 1.0, None, ALU.add))
                    own.wait()
                    own(V.reciprocal(f, f))
                    own.wait()
                    own(V.scalar_tensor_tensor(k, k, lbc[:, 1, a:a + 1], f, ALU.mult, ALU.mult))
                    own.wait()
                    own(V.tensor_scalar(f, f, lbc[:, 1, a:a + 1], lbc[:, 0, a:a + 1], ALU.mult, ALU.add))
                    own.wait()
                    V.tensor_scalar(f, f, MIN_FORGET, None, ALU.max).then_inc(S["k_up"], 4)

                def gate_q(a):
                    e = q_tmp[:, a, :]
                    dve.wait_ge(S["e_q"], a + 1)
                    own(V.tensor_scalar(e, e, 1.0, None, ALU.add))
                    own.wait()
                    own(V.reciprocal(e, e))
                    own.wait()
                    V.tensor_tensor(qq[:, a, :], qq[:, a, :], e, ALU.mult).then_inc(S["q_up"], 1)

                def gate_g(a):
                    e = g_tmp[a % 2][:]
                    dve.wait_ge(S["e_g"], a + 1)
                    own(V.tensor_scalar(e, e, 1.0, None, ALU.add))
                    own.wait()
                    own(V.reciprocal(e, e))
                    own.wait()
                    V.tensor_tensor(gg[:, a, :], gg[:, a, :], e, ALU.mult).then_inc(S["g_gated"], 1)

                def level(lv):
                    for a in range(HR):
                        dve.wait_ge(S["lv"], HR * lv + a + 1)
                        V.copy_predicated(out=sc[:, a, :].rearrange("p (c t) -> p c t", c=CH),
                                          mask=masks[:, lv, :].unsqueeze(1).broadcast_to([P, CH, P]),
                                          data=ps[:, 4 + a % 3, :].rearrange("p (c t) -> p c t", c=CH)).then_inc(S["sc_set"], 1)
                        if lv == 0:
                            V.tensor_tensor(qq[:, a, :], qq[:, a, :], zf[:, a, :], ALU.mult).then_inc(S["q_up"], 1)
                        else:
                            h = 1 << (lv - 1)
                            wd = TT if h <= 4 else TP
                            n = wd // (2 * h)
                            if lv > 1:
                                dve.wait_ge(S["k_up"], 2 * (HR * lv + a + 1))
                            f = tot[lv - 1][:, a, 0:wd // h].rearrange("p (n two) -> p n two", two=2)
                            q = qq[:, a, 0:wd].rearrange("p (n two h) -> p n two h", two=2, h=h)[:, :, 1, :]
                            V.tensor_tensor(q, q, f[:, :, 0].unsqueeze(2).broadcast_to([P, n, h]),
                                            ALU.mult).then_inc(S["q_up"], 1)
                    if lv < S_LEVELS:
                        V.copy_predicated(out=scs[0:TS], mask=masks[0:TS, lv, 0:TS].unsqueeze(1).broadcast_to([TS, HR, TS]),
                                          data=ps[0:TS, 7, 0:HR * TS].rearrange("p (a t) -> p a t", a=HR))\
                            .then_inc(S["scs_set"], 1)
                    dve.wait_ge(S["sc_set"], HR * lv + 2 * HR)
                    dve.wait_ge(S["q_up"], HR * lv + 2 * HR)
                    if lv < S_LEVELS:
                        dve.wait_ge(S["scs_set"], lv + 2)

                tot = [zf, f2[:], f4[:]] + [f[:] for f in f_small]
                for b in range(BLK_OUT):
                    made = MADE[b]
                    dve.wait_ge(S["blk"], b + 1)
                    if B_F <= made < B_F + HR:
                        V.tensor_scalar(halves(proj[:, made, :]), pair_of(b % 2), -80.0, None, ALU.max).then_inc(S["free"], 1)
                    else:
                        V.tensor_copy(halves(proj[:, made, :]), pair_of(b % 2)).then_inc(S["free"], 1)
                    if 1 <= b <= HR:
                        gate_f(b - 1)
                    elif HR < b <= 2 * HR:
                        gate_q(b - 1 - HR)
                    elif b == 2 * G_LV:
                        dve.wait_ge(S["v_t"], CH + 1)
                        V.memset(sc[:], 0.0).then_inc(S["sc_set"], HR)
                        V.memset(scs[0:TS], 0.0).then_inc(S["scs_set"], 1)
                        dve.wait_ge(S["sc_set"], HR)
                        dve.wait_ge(S["scs_set"], 1)
                        dve.wait_ge(S["q_up"], HR)
                    if b > 2 * G_LV and b % 2:
                        level(b // 2 - G_LV)
                    if made in (B_G + 1, B_G + 2):
                        gate_g(made - B_G - 1)
                    if b == BLK_OUT - HR - 1:
                        dve.wait_ge(S["k_up"], 2 * HR * 5)

                dve.wait_ge(S["k_up"], 2 * HR * (LEVELS + 1))
                for a in range(HR):
                    dve.wait_ge(S["u_done"], a + 1)
                    bank = (a + 1) % 4
                    own(V.tensor_copy(states[:, a, 0, :], ps[:, bank, 0:P]))
                    for c in range(1, CH):
                        own.wait()
                        ins = V.scalar_tensor_tensor(states[:, a, c, :], states[:, a, c - 1, :], f_small[4][:, a, c:c + 1],
                                                     ps[:, bank, c * P:c * P + P], ALU.mult, ALU.add)
                        if c < CH - 1:
                            own(ins)
                        else:
                            ins.then_inc(S["st_done"], 1)
                for a in range(HR):
                    if a % 2 == 0:
                        gate_g(2 + a // 2)
                    s = s_in[a % 2]
                    dve.wait_ge(S["su_done"], a + 1)
                    own(V.tensor_tensor(s[:], s[:], f_small[0][:, a, TP // TB:TT // TB].unsqueeze(2).broadcast_to([P, NB, P]),
                                        ALU.mult))
                    own.wait()
                    V.tensor_tensor(s[:].rearrange("p b v -> p (b v)"), s[:].rearrange("p b v -> p (b v)"),
                                    ps[:, 2:4, :].rearrange("p a b -> p (a b)"), ALU.add).then_inc(S["s_new"], 1)
                dve.wait_ge(S["o_there"], HR + 1)
                V.tensor_tensor(o_raw[:, :, TP:TT], o_raw[:, :, TP:TT], ps[:, 1, 0:HR * TS].rearrange("p (a t) -> p a t", a=HR),
                                ALU.add).then_inc(S["os_set"], 1)
                def rec(a):
                    if a:
                        dve.wait_ge(S["r_hi"], a)
                        if a == 1:
                            for s in range(2):
                                dve.wait_ge(S[f"s_out{s}"], 32)
                        V.tensor_tensor(hl[:, a - 1, :], t3[:], hh[:, a - 1, :].bitcast(F32), ALU.subtract).then_inc(S["r_lo"], 1)
                        dve.wait_ge(S["r_lo"], a)
                    if a < HR:
                        dve.wait_ge(S["r_root"], a + 1)
                        own(V.reciprocal(t2[:], t2[:]))
                        own.wait()
                        own(V.scalar_tensor_tensor(t3[:], o_raw[:, a, :], prm[:, 4 * KC + a:4 * KC + a + 1], t2[:],
                                                   ALU.mult, ALU.mult))
                        own.wait()
                        V.tensor_tensor(t3[:], t3[:], gg[:, a, :], ALU.mult).then_inc(S["r_scaled"], 1)

                gain = prm[:, 4 * KC + HR:4 * KC + HR + HP]

                def att_rest(a, n):
                    dve.wait_ge(S["a_hi"], a + 1)
                    V.tensor_tensor(hl[:, HR + a, 0:TP], t3[:, 0:TP], hh[:, HR + a, 0:TP].bitcast(F32),
                                    ALU.subtract).then_inc(S["a_lo"], 1)
                    dve.wait_ge(S["a_lo"], n + 1)

                def att(a):
                    if 0 < a < HP - 1:
                        att_rest(a - 1, a - 1)
                    dve.wait_ge(S["a_root"], a + 1)
                    own(V.reciprocal(t2[:, 0:TP], t2[:, 0:TP]))
                    own.wait()
                    V.scalar_tensor_tensor(t3[:, 0:TP], ao[:, a, 0:TP], gain[:, a:a + 1], t2[:, 0:TP],
                                           ALU.mult, ALU.mult).then_inc(S["a_scaled"], 1)

                def sam_norm():
                    att_rest(HP - 2, HP - 2)
                    dve.wait_ge(S["n_root"], 1)
                    own(V.reciprocal(t2[:, 0:HP * TS], t2[:, 0:HP * TS]))
                    own.wait()
                    for a in range(HP):
                        cols = slice(a * TS, a * TS + TS)
                        ins = V.scalar_tensor_tensor(t3[:, cols], ao[:, a, TP:TT], gain[:, a:a + 1], t2[:, cols],
                                                     ALU.mult, ALU.mult)
                    ins.then_inc(S["n_scaled"], 1)

                def sam(p2, k):
                    m = mx[:, 2, :]
                    if k == 0:
                        if p2 == 0:
                            dve.wait_ge(S["ts_in"], 16 * 4 * HA)
                            dve.wait_ge(S["r_scaled"], HR)
                        dve.wait_ge(S["ss_done"], p2 + 1)
                        V.tensor_tensor(ps_s[:, 0:PAST], ps[:, 7, 0:PAST], ts_cache[:], ALU.add).then_inc(S["ss_max"], 1)
                        V.tensor_tensor(ps_s[:, PAST:PAST + TS], ps[:, 7, PAST:PAST + TS],
                                        ts_new[:, p2 * TS:p2 * TS + TS], ALU.add).then_inc(S["ss_max"], 1)
                        dve.wait_ge(S["ss_max"], 4 * p2 + 2)
                        V.reduce_max(m[:, 0:1], ps_s[:], AX.X).then_inc(S["ss_max"], 1)
                        dve.wait_ge(S["ss_max"], 4 * p2 + 3)
                        V.tensor_scalar(m[:, 1:2], m[:, 0:1], -0.125, None, ALU.mult).then_inc(S["ss_max"], 1)
                        dve.wait_ge(S["sp_exp"], p2 + 1)
                        own(V.reciprocal(m[:, 3:4], m[:, 2:3]))
                        own.wait()
                        V.tensor_scalar(ps_s[:], ps_s[:], m[:, 3:4], None, ALU.mult).then_inc(S["sp_norm"], 1)
                    if k == 2:
                        dve.wait_ge(S["spv_done"], p2 + 1)
                        V.tensor_tensor(mo[:].rearrange("p (h d) -> p h d", h=HA),
                                        ps[:, 7, :].rearrange("p (h d) -> p h d", h=HA),
                                        head_mask.unsqueeze(2).broadcast_to([P, HA, DH]), ALU.mult).then_inc(S["mo_set"], 1)

                steps = {"rec": rec, "att": att, "sam": sam, "sam_norm": sam_norm}

                def beside(h, place_):
                    if (h, place_) in BESIDE:
                        name, *which = BESIDE[h, place_]
                        steps[name](*which)

                for j in range(HP):
                    qv = qbig[:, j, :].rearrange("p (b h t) -> p b h t", b=NB, h=HA)
                    for s in range(2):
                        r = slice(DH * s, DH * s + DH)
                        ins = V.tensor_copy(qv[r, :, 2 * j + s, :],
                                            proj[r, B_QA + j, TP:TT].rearrange("p (b t) -> p b t", b=NB))
                ins.then_inc(S["qb"], 1)
                rec(0)
                for h in range(HA + 2):
                    if h < HA:
                        pr, m = prob[h % 2], mx[:, h % 2, :]
                        if h % HP == 0:
                            dve.wait_ge(S[f"b_in{h // HP}"], 16)
                        if h >= 2:
                            dve.wait_ge(S["p_t"], 3 * (h - 1))
                        for n, (i, (bank, c0)) in enumerate(s_at.items()):
                            if n < CH - 1:
                                dve.wait_ge(S["s_done"], (CH - 1) * h + n + 1)
                            V.tensor_tensor_reduce(out=pr[:, tri[i]:tri[i + 1]], in0=ps[:, bank, c0:c0 + (i + 1) * P],
                                                   in1=bias[h // HP][:, h % HP, (CH - 1 - i) * P:TP], scale=1.0, scalar=-3.0e38,
                                                   op0=ALU.add, op1=ALU.max, accum_out=m[:, i:i + 1]).then_inc(S["s_max"], 1)
                        dve.wait_ge(S["s_max"], (CH + 1) * h + CH)
                        V.tensor_scalar(m[:, 4:8], m[:, 0:4], -0.125, None, ALU.mult).then_inc(S["s_max"], 1)
                    beside(h, 0)
                    if 0 < h <= HA:
                        g = h - 1
                        pr, m = prob[g % 2], mx[:, g % 2, :]
                        dve.wait_ge(S["p_exp"], CH * (g + 1))
                        own(V.reciprocal(m[:, 12:16], m[:, 8:12]))
                        own.wait()
                        for i in range(CH):
                            V.tensor_scalar(pr[:, tri[i]:tri[i + 1]], pr[:, tri[i]:tri[i + 1]], m[:, 12 + i:13 + i], None,
                                            ALU.mult).then_inc(S["p_norm"], 1)
                    beside(h, 1)
                    beside(h, 2)
                dve.wait_ge(S["n_hi"], 1)
                V.tensor_tensor(hl[:, HR:HR + HP, TP:TT], t3[:, 0:HP * TS].rearrange("p (a t) -> p a t", a=HP),
                                hh[:, HR:HR + HP, TP:TT].bitcast(F32), ALU.subtract).then_inc(S["a_lo"], 1)
                dve.wait_ge(S["a_lo"], HP)
                att(HP - 1)
                att_rest(HP - 1, HP)

                def leave(b, add):
                    i, k, before = b
                    dve.wait_ge(S["blk"], 4 * i + (k + 1 + before))
                    dst = acc[:, bass.ds(4 * i + k, 1), :].rearrange("p o (a t) -> p (o a) t", a=2)
                    if add:
                        V.tensor_tensor(dst, dst, pair_of(k % 2), ALU.add).then_inc(S["free"], 1)
                    else:
                        V.tensor_copy(dst, pair_of(k % 2)).then_inc(S["free"], 1)

                for c in range(KC):
                    leave((c // 4, c % 4, BLK_OUT), False)
                    sum_squares(1, c)
                norm_apply(1, prm[:, KC:2 * KC], True)
                norm_apply(2, prm[:, 2 * KC:3 * KC], False)

                def up(q):
                    with own.loop(0, G_UP // 2, 2 * 4) as i:
                        for k in range(4):
                            b = q * BLK_Q + BLK_MLP
                            dve.wait_ge(S["blk"], 4 * i + (k + 1) + b)
                            V.tensor_scalar(halves(t1[:]), pair_of(k % 2), 0.0, None, ALU.max).then_inc(S["free"], 1)
                            dve.wait_ge(S["free"], 4 * i + (k + 3) + b)
                            own(V.tensor_tensor(t2[:], t1[:], t1[:], ALU.mult))
                            own.wait()
                            u = uh[:, bass.ds(4 * i + k, 1), :].rearrange("p o t -> p (o t)")
                            own(V.tensor_copy(u, t2[:]))
                            own.wait()
                            u2 = ul[:, bass.ds(4 * i + k, 1), :].rearrange("p o t -> p (o t)")
                            V.tensor_tensor(u2, t2[:], u.bitcast(F32), ALU.subtract).then_inc(S["u_set"], 1)
                            dve.wait_ge(S["u_set"], 4 * i + (k + 1) + q * KC)

                def down(q, add):
                    with dve.Fori(0, G_DOWN // 2) as i:
                        for k in range(4):
                            leave((i, k, q * BLK_Q + (BLK_MLP + 2 * G_UP)), add)

                up(0)
                down(0, False)
                n0 = own.n
                per = 2 * 8
                with dve.Fori(1, NQ - 1) as q:
                    own.n = n0 + (q - 1) * per
                    up(q)
                    down(q, True)
                own.n = n0 + (NQ - 2) * per
                up(NQ - 1)
                for c in range(KC):
                    leave((c // 4, c % 4, 2 * (G_ALL - G_DOWN)), True)
                    sum_squares(3, c)
                norm_apply(3, prm[:, 3 * KC:4 * KC], True)

        nc.sync.sem_clear(range(nums[0], nums[-1] + 1))
        nc.all_engine_barrier()

    y_out = sem("y_out")
    with nc.Block() as block:
        @block.sync
        def _(sp):
            sp.dma_start(yT, x[:]).then_inc(y_out, 16)
            sp.wait_ge(y_out, 16)
    ctx.close()


def kernel(x_prompt, x_sample, state_hgrn, cache_k, cache_v, rel_bias, lb_raw, w_in, w_out, w_up, w_down,
           g_mix_pre, g_mix_post, g_mlp_pre, g_mlp_post, g_rec_out, g_attn_out):
    import concourse.bacc as bacc
    from concourse.bass_utils import run_bass_kernel_spmd

    f = lambda a: np.asarray(a)
    L = DEPTH
    x = np.concatenate([f(x_prompt).reshape(TP, D), f(x_sample).reshape(TS, D)], 0)
    blocks = lambda m, n: m.reshape(n, P, -1).transpose(1, 0, 2)

    def groups(m):
        return m.reshape(KC, P, -1, GC).transpose(2, 1, 0, 3).reshape(-1, P, KC * GC)

    order = [1, 0, 2, 6, 5, 4, 3]
    ws = []
    for l in range(L):
        wi = f(w_in)[l]
        parts = [groups(np.concatenate([wi[:, 512 * o:512 * o + 512] for o in order], 1)), groups(f(w_out)[l])]
        for q in range(NQ):
            n = FF // NQ
            parts += [groups(f(w_up)[l][:, q * n:q * n + n]), groups(f(w_down)[l][q * n:q * n + n, :])]
        ws += parts
    cst, masks, rel = constants()
    cols = lambda g, n: f(g).reshape(L, n, P).transpose(0, 2, 1)
    ins = {
        "xT": blocks(x.T, KC),
        "w": np.concatenate(ws, 0),
        "par": np.concatenate([cols(g, KC) for g in (g_mix_pre, g_mix_post, g_mlp_pre, g_mlp_post)]
                              + [cols(g_rec_out, HR), cols(g_attn_out, HP)], 2),
        "lbr": f(lb_raw).reshape(L, HR, P).transpose(2, 0, 1),
        "relb": f(rel_bias),
        "s0": f(state_hgrn).transpose(0, 2, 3, 1, 4).reshape(L * HR, P, NB, P),
        "kcT": f(cache_k).reshape(L * NB, PAST, HP, P).transpose(0, 3, 2, 1),
        "vc": f(cache_v).reshape(L * NB, 2, P, 512).transpose(0, 2, 1, 3),
        "cst": cst, "msk": masks, "rel": rel,
    }
    ins = {k: np.ascontiguousarray(v) for k, v in ins.items()}
    outs = {"yT": (P, KC, TT), "sp": (L, P, HR, P), "kT": (L, P, HP, TT), "vo": (L, TT, 512), "ss": (L * HR, P, NB, P)}
    nc = bacc.Bacc("TRN2", target_bir_lowering=False, num_devices=1)
    i_aps = [nc.dram_tensor(k, v.shape, mybir.dt.from_np(v.dtype), kind="ExternalInput").ap() for k, v in ins.items()]
    o_aps = [nc.dram_tensor(k, s, F32, kind="ExternalOutput").ap() for k, s in outs.items()]
    scratch = nc.dram_tensor("rel_scratch", (P, HA, NREL), F32)
    build(nc, *i_aps, *o_aps, scratch)
    r = run_bass_kernel_spmd(nc, [ins], core_ids=[0]).results[0]
    y = r["yT"].transpose(1, 0, 2).reshape(D, TT).T
    k_new = r["kT"].transpose(0, 3, 2, 1).reshape(L, TT, HA, DH)
    v_new = r["vo"].reshape(L, TT, HA, DH)
    return (y[:TP].reshape(1, TP, D), y[TP:].reshape(NB, TB, D),
            r["sp"].transpose(0, 2, 1, 3).reshape(L, 1, HR, P, P),
            k_new[:, :TP].reshape(L, 1, TP, HA, DH), v_new[:, :TP].reshape(L, 1, TP, HA, DH),
            r["ss"].reshape(L, HR, P, NB, P).transpose(0, 3, 1, 2, 4),
            k_new[:, TP:].reshape(L, NB, TB, HA, DH), v_new[:, TP:].reshape(L, NB, TB, HA, DH))
```

```python
from contextlib import ExitStack, contextmanager

import numpy as np
import concourse.bass as bass
from concourse import mybir

F32 = mybir.dt.float32
F32R = mybir.dt.float32r
U8 = mybir.dt.uint8
ALU = mybir.AluOpType
ACT = mybir.ActivationFunctionType
AX = mybir.AxisListType

P = 128
DEPTH, D, FF = 2, 1024, 4096
TP, NB, TB = 512, 8, 8
TS = NB * TB
TT = TP + TS
HT = TT // 2
KC = D // P
HR, HA, DH = 4, 8, 64
HP = HA // 2
PAST = 256
CH = TP // P
NEG = -1.0e30
EPS = 1.0e-6
MIN_FORGET = 1.0e-30
WINDOWS = ((128, 1), (512, 4), (2048, 16))
NBUCKET, MAXDIST = 32, 2048

GC = 256
G_IN, G_OUT = 14, 4
NQ = 4
G_UP = G_DOWN = FF // NQ // GC
G_ALL = G_IN + G_OUT + NQ * (G_UP + G_DOWN)
BLK_OUT = 2 * G_IN
BLK_MLP = BLK_OUT + 2 * G_OUT
BLK_Q = 2 * (G_UP + G_DOWN)
B_I, B_F, B_Q, B_V, B_K, B_QA, B_G = 0, 4, 8, 12, 16, 20, 24
MADE = [b + a for b in (B_F, B_Q, B_I, B_V, B_K, B_QA, B_G) for a in range(4)]
G_LV = 6
LEVELS = 8
S_LEVELS = 4
NREL = 640
N_PAR = 4 * KC + HR + HP

BESIDE = {(0, 0): ("rec_s", 1), (1, 0): ("sam", 0, 0), (1, 2): ("sam", 0, 1), (2, 0): ("sam", 0, 2),
          (2, 1): ("sam", 0, 3), (2, 2): ("sam", 1, 0), (3, 1): ("sam", 1, 1), (3, 2): ("sam", 1, 2),
          (4, 0): ("sam", 1, 3), (4, 1): ("att", 0, 0), (4, 2): ("att", 0, 1), (5, 0): ("sam", 2, 0),
          (5, 2): ("sam", 2, 1), (6, 0): ("sam", 2, 2), (6, 1): ("sam", 2, 3), (6, 2): ("att", 1, 0),
          (7, 1): ("att", 1, 1), (7, 2): ("sam", 3, 0), (8, 1): ("sam", 3, 1), (8, 2): ("sam", 3, 2),
          (9, 0): ("sam", 3, 3), (9, 1): ("att", 2, 0), (9, 2): ("att", 2, 1), (10, 0): ("sam_norm", 0),
          (10, 1): ("sam_norm", 1)}


def rel_buckets(dist):
    exact = NBUCKET // 2
    d = np.maximum(dist, exact).astype(np.float32)
    large = exact + (np.log(d / exact) / np.float32(np.log(MAXDIST / exact)) * (NBUCKET - exact)).astype(np.int32)
    return np.where(dist < exact, dist, np.minimum(large, NBUCKET - 1))


def constants():
    eye = np.eye(P, dtype=np.float32)
    half = np.kron(np.eye(2), np.ones((DH, DH))).astype(np.float32)
    row = np.arange(P)
    head_of_row = ((row % 64) // TB)[:, None] == np.arange(HA)[None]
    tok_of_row = (row // 64 * TB + row % TB)[:, None] == np.arange(2 * TB)[None]
    seq_of_tok = (row // TB)[:, None] == np.arange(NB)[None]
    cst = np.concatenate([eye, half, head_of_row, tok_of_row, seq_of_tok], 1).astype(np.float32)
    s, t = np.arange(P)[:, None], np.arange(P)[None]
    masks = [s == t]
    for lv in range(1, LEVELS):
        h = 1 << (lv - 1)
        masks.append((s // (2 * h) == t // (2 * h)) & (s // h % 2 == 0) & (t // h % 2 == 1))
    masks = np.stack(masks, 1).astype(np.float32)
    dist = 511 - np.arange(NREL)
    count = sum(((dist >= 0) & (dist % d == 0) & (dist <= w)).astype(int) for w, d in WINDOWS)
    rel = np.zeros((NBUCKET + 1, NREL), np.float32)
    rel[rel_buckets(np.maximum(dist, 0)), np.arange(NREL)] = 8.0 * (count > 0)
    rel[NBUCKET] = np.where(count > 0, 8.0 * np.log(np.maximum(count, 1)), NEG)
    return cst, masks, rel


class Steps:

    def __init__(self, eng, sem):
        self.eng, self.sem, self.n = eng, sem, 0

    def __call__(self, ins):
        ins.then_inc(self.sem, 1)
        self.n = self.n + 1

    def wait(self):
        self.eng.wait_ge(self.sem, self.n)

    @contextmanager
    def loop(self, a, b, per):
        start = self.n
        with self.eng.Fori(a, b) as i:
            self.n = start + (i - a) * per
            yield i
        self.n = start + (b - a) * per


def build(nc, xT, w, par, lbr, relb, s0, kcT, vc, cst_d, msk_d, rel_d, yT, sp_o, kT_o, v_o, ss_o, rel_row, rel_scr):
    ctx = ExitStack()
    at = [16512]

    def place(name, shape, dt=F32, offset=None):
        size = int(np.prod(shape[1:])) * (1 if dt == U8 else 4)
        if offset is None:
            offset = at[0]
            at[0] += (size + 31) // 32 * 32
        return nc.alloc_sbuf_tensor_at(name, list(shape), dt, offset=offset)

    FB = TT * 4
    x = place("x", [P, KC, TT])
    root = place("root", [P, 24])
    inv = place("inv", [P, 24])
    o_hh = at[0]
    hh = place("h_high", [P, KC, TT], F32R)
    o_hl = at[0]
    hl = place("h_rest", [P, KC, TT], F32R)
    raw = [place(f"w_raw{s}", [P, KC, GC]) for s in range(2)]
    whi = [place(f"w_high{s}", [P, KC, GC], F32R) for s in range(2)]
    wlo = [place(f"w_rest{s}", [P, KC, GC], F32R) for s in range(2)]
    t1, o_t2 = place("t1", [P, TT]), at[0]
    t2, t3 = place("t2", [P, TT]), place("t3", [P, TT])
    cst = place("cst", [P, 288])
    ones = place("ones", [P, P])
    masks = place("masks", [P, LEVELS, P], U8)
    ts_cache = place("ts_cache", [P, PAST])
    ts_new = place("ts_new", [P, HP * (TS + 2 * TB)])
    qbig = place("qbig", [P, HP, NB * 64])
    prm = place("prm", [P, N_PAR])
    lb = place("lb", [P, DEPTH, HR])
    lbc = place("lbc", [P, 2, HR])
    eps = place("eps", [P, 1])
    mx = place("mx", [P, 3, 16])
    f_small = [place(f"f_tot{8 << i}", [P, HR, (TT if i == 0 else TP) // (8 << i)]) for i in range(5)]
    o_proj = at[0]
    proj = place("proj", [P, 28, TT])
    o_v = at[0]
    vt = place("v_tok", [P, CH + 1, 512])
    o_kb = at[0]
    kb = place("k_dec", [P, HR, TT])
    assert at[0] <= 229344, at[0]

    ident = cst[:, 0:P]
    half_ones = cst[:, P:2 * P]
    head_mask = cst[:, 256:264]
    tok_sel = cst[:, 264:280]
    seq_mask = cst[:, 280:288]

    va = place("va_tok", [P, CH + 1, 512], offset=o_v)
    g_tmp = [t1, t3]
    states = place("states", [P, HR, CH, P], offset=o_hh)
    f2 = place("f_tot2", [P, HR, TT // 2], offset=o_proj + B_G * FB)
    f4 = place("f_tot4", [P, HR, TT // 4], offset=o_proj + (B_G + 2) * FB)
    kt = place("k_tok", [P, HR, TP], offset=o_hh + 4 * FB)
    kts = place("ks_tok", [P, HR * P], offset=o_t2)
    s_in = [place(f"s_in{s}", [P, NB, P], offset=o + 4096 * (s % 2))
            for s, o in enumerate((o_hl + 4 * FB, o_hl + 4 * FB, o_hh + 4 * FB, o_hh + 4 * FB))]
    sc = place("sc", [P, HR, TP], offset=o_proj + B_I * FB)
    scs = place("scs", [P, HR, TS], offset=o_proj + B_I * FB + 4 * HR * TP)
    v_exp = [place(f"v_exp{s}", [P, NB, P], offset=o_hl + 4096 * s) for s in range(2)]
    ao = place("ao", [P, HP, TT], offset=o_hl + 4 * FB)
    o_raw = proj[:, B_F:B_F + HR, :]
    rs = place("rs", [P, HR * TS], offset=o_t2)
    o_sq = place("o_sq", [P, HR, TT], offset=o_kb)
    q_tmp = proj[:, B_G:B_G + HR, :]
    bias = [place("bias0", [P, HA // 2, TP], offset=o_hh + 4 * FB),
            place("bias1", [P, HA // 2, TP], offset=o_proj + B_F * FB)]
    o_reg = [o_proj + B_Q * FB, o_kb, o_proj + B_V * FB, o_proj + B_I * FB]
    tri = [P * i * (i + 1) // 2 for i in range(CH + 1)]
    prob = [place(f"prob{s}", [P, tri[CH]], offset=o_reg[s]) for s in range(2)]
    pt = [place(f"prob_t{s}", [P, tri[CH]], offset=o_reg[2 + s]) for s in range(2)]
    trj = [tri[CH] - tri[CH - j] for j in range(CH)]
    kc = [place(f"kc{s}", [P, HP, PAST], offset=o_reg[s] + 4 * tri[CH]) for s in range(2)]
    vcs = [place(f"vc{s}", [P, 2, 512], offset=o_reg[2 + s] + 4 * tri[CH]) for s in range(2)]
    ps_s = place("probs_s", [P, PAST + TS], offset=o_proj + B_G * FB)
    pts = place("probs_st", [P, 3 * P], offset=o_proj + (B_G + 1) * FB)
    mo = place("mo", [P, 512], offset=o_proj + (B_G + 2) * FB)
    s_at = {3: (2, 0), 1: (1, 0), 0: (0, 0), 2: (0, P)}
    acc = proj[:, 0:KC, :]
    uh = place("u_high", [P, KC, TT], F32R, offset=o_proj + 8 * FB)
    ul = place("u_rest", [P, KC, TT], F32R, offset=o_proj + 16 * FB)
    ys = proj[:, 8:16, :]
    ssq = proj[:, 24, :]
    sqs = place("squares", [P, KC, TT], offset=o_v)
    rel_sb = place("rel_sb", [P, NREL], offset=o_proj)
    rel_r = place("rel_r", [P, NREL], offset=o_proj + 2 * FB)
    rel_l = place("rel_l", [P, HA], offset=o_proj + 4 * FB)
    masks_f = place("masks_f", [P, LEVELS, P], offset=o_proj + 6 * FB)

    ps = ctx.enter_context(nc.psum_tensor("ps", [P, 8, 512], F32))

    def sem(name):
        return ctx.enter_context(nc.semaphore(name))

    c_in, c_tab = sem("c_in"), sem("c_tab")
    c_mm, c_cp, c_set, c_lb, c_exp = sem("c_mm"), sem("c_cp"), sem("c_set"), sem("c_lb"), sem("c_exp")
    c_x, c_row = sem("c_x"), sem("c_row")
    w_ahead, hi_ahead, lo_ahead = [sem("w_ahead0"), sem("w_ahead1")], sem("hi_ahead"), sem("lo_ahead")
    with nc.Block() as block:
        @block.sync
        def _(sp):
            for dst, src in ((rel_r[0:NBUCKET + 1, :], rel_d), (rel_l[0:NBUCKET, :], relb), (lb[:], lbr),
                             (masks_f[:], msk_d), (cst[:], cst_d)):
                sp.dma_start(dst, src).then_inc(c_in, 16)
            for s in range(2):
                if s:
                    sp.dma_start(x[:], xT).then_inc(c_x, 16)
                sp.dma_start(raw[s][:].rearrange("p a b -> p (a b)"),
                             w[s:s + 1].rearrange("o p n -> p (o n)")).then_inc(w_ahead[s], 16)
            sp.wait_ge(c_cp, 2)
            sp.dma_start(rel_row.ap(), rel_sb[0:HA, :]).then_inc(c_row, 16)
            sp.wait_ge(c_row, 16)
            sp.dma_start(rel_scr.ap().rearrange("p h n -> p (h n)"),
                         bass.AP(rel_row, 0, [[0, P], [1, HA * NREL]])).then_inc(c_tab, 16)

        @block.gpsimd
        def _(pool):
            for n, (tile, value) in enumerate(((ts_new[:], NEG), (qbig[:], 0.0), (ones[:], 1.0), (eps[:], EPS),
                                               (rel_l[NBUCKET:NBUCKET + 1, :], 1.0))):
                if n:
                    pool.wait_ge(c_set, n)
                nc.gpsimd.memset(tile, value).then_inc(c_set, 1)
            pool.wait_ge(c_set, 5)
            pool.wait_ge(hi_ahead, 1)
            nc.gpsimd.tensor_tensor(wlo[0][:], raw[0][:], whi[0][:].bitcast(F32), ALU.subtract).then_inc(lo_ahead, 1)
            pool.wait_ge(lo_ahead, 1)

        @block.tensor
        def _(pe):
            pe.wait_ge(c_in, 80)
            pe.wait_ge(c_set, 5)
            for n, cols in enumerate((slice(0, 512), slice(512, NREL))):
                nc.tensor.matmul(ps[0:HA, n, 0:cols.stop - cols.start], rel_l[0:NBUCKET + 1, :],
                                 rel_r[0:NBUCKET + 1, cols], start=True, stop=True).then_inc(c_mm, 1)

        @block.scalar
        def _(act):
            act.wait_ge(c_lb, 2)
            nc.scalar.activation(lb[:], lb[:], ACT.Exp).then_inc(c_exp, 1)
            act.wait_ge(w_ahead[0], 16)
            nc.scalar.activation(whi[0][:], raw[0][:], ACT.Copy).then_inc(hi_ahead, 1)
            act.wait_ge(c_x, 16)
            for c in range(KC):
                nc.scalar.activation(sqs[:, c, :], x[:, c, :], ACT.Square)

        @block.vector
        def _(dve):
            own = Steps(dve, c_lb)
            dve.wait_ge(c_in, 80)
            own(nc.vector.tensor_tensor(lbc[:, 0, :], lb[:, 0, :], lb[:, 1, :], ALU.max))
            own.wait()
            own(nc.vector.tensor_tensor(lb[:], lb[:], lbc[:, 0:1, :].broadcast_to([P, DEPTH, HR]), ALU.subtract))
            dve.wait_ge(c_exp, 1)
            own(nc.vector.tensor_tensor(lbc[:, 0, :], lb[:, 0, :], lb[:, 1, :], ALU.add))
            own.wait()
            own(nc.vector.reciprocal(lbc[:, 1, :], lbc[:, 0, :]))
            own.wait()
            own(nc.vector.tensor_tensor(lb[:], lb[:], lbc[:, 1:2, :].broadcast_to([P, DEPTH, HR]), ALU.mult))
            own.wait()
            own(nc.vector.tensor_tensor(lbc[:, 0, :], lb[:, 0, :], lb[:, 1, :], ALU.add))
            own.wait()
            own(nc.vector.tensor_tensor(lb[:, 1, :], lbc[:, 0, :], lb[:, 0, :], ALU.subtract))
            own.wait()
            own(nc.vector.memset(lb[:, 0, :], 0.0))
            own(nc.vector.tensor_copy(masks[:], masks_f[:]))
            for n, cols in enumerate((slice(0, 512), slice(512, NREL))):
                dve.wait_ge(c_mm, n + 1)
                nc.vector.tensor_copy(rel_sb[0:HA, cols], ps[0:HA, n, 0:cols.stop - cols.start]).then_inc(c_cp, 1)
            own.wait()
            dve.wait_ge(c_cp, 2)

    lay = ["w_in0", "w_in1", "w_hi", "w_ready", "blk", "free", "prm_in",
           "sq", "ssq", "quad", "ms", "root", "inv", "spread", "scaled", "h_hi", "h_even", "h_odd", "xr", "xr_odd", "dv",
           "e_f", "f_inv", "e_q", "e_g",
           "v_t", "v_there", "lv", "sc_set", "scs_set", "q_up", "k_up",
           "k_t", "k_there", "u_done", "st_done", "o_done", "o_there", "os_set",
           "s0_in0", "s0_in1", "s0_in2", "s0_in3", "s_out", "v_wide", "su_done", "s_new",
           "r_sq", "r_ms", "r_root", "r_inv", "r_spread", "r_scaled", "r_hi", "r_lo", "rs_mul",
           "va_t", "va_there", "b_in0", "b_in1", "qb", "s_done", "s_max", "p_exp", "p_norm", "p_t", "pt_there",
           "pv_done", "ao_there",
           "kc_in0", "kc_in1", "vc_in0", "vc_in1", "ss_done", "ss_max", "sp_exp", "sp_norm", "sp_t", "spt_there",
           "spv_done", "mo_set", "sel_done",
           "a_sq", "a_ms", "a_root", "a_inv", "a_spread", "a_scaled", "a_hi", "a_lo", "u_set",
           "g_gated", "so_there", "n_sq", "n_ms", "n_root", "n_inv", "n_spread", "n_scaled", "n_hi", "ts_in", "st_out", "k_out", "v_out0", "v_out1"]
    S = {n: sem(n) for n in lay}
    nums = [S[n].num for n in lay]
    assert nums == list(range(nums[0], nums[0] + len(nums)))

    def pair_of(m, part=slice(0, P)):
        return ps[part, 2 * m:2 * m + 2, 0:HT]

    def halves(ap):
        return ap.rearrange("p (a t) -> p a t", a=2)

    with nc.Fori(0, DEPTH) as l:
        with nc.Block() as block:
            @block.sync
            def _(sp):
                def load(g, s):
                    sp.dma_start(raw[s][:].rearrange("p a b -> p (a b)"),
                                 w[bass.ds(l * G_ALL + g, 1)].rearrange("o p n -> p (o n)")).then_inc(S[f"w_in{s}"], 16)

                with sp.Fori(1, G_ALL // 2) as i:
                    for s in range(2):
                        sp.wait_ge(S["w_ready"], 2 * i + s - 1)
                        load(2 * i + s, s)
                for s in range(2):
                    sp.wait_ge(S["w_ready"], G_ALL - 1 + s)
                    sp.dma_start(raw[s][:].rearrange("p a b -> p (a b)"),
                                 w[bass.ds((DEPTH - 1 - l) * G_ALL + s, 1)].rearrange("o p n -> p (o n)")).then_inc(w_ahead[s], 16)

            @block.gpsimd
            def _(pool):

                def rest(a, b):
                    with pool.Fori(a, b) as i:
                        for s in range(2):
                            pool.wait_ge(S["w_hi"], 2 * i + s + 1)
                            nc.gpsimd.tensor_tensor(wlo[s][:], raw[s][:], whi[s][:].bitcast(F32),
                                                    ALU.subtract).then_inc(S["w_ready"], 1)

                def rest_of(g, s):
                    pool.wait_ge(S["w_hi"], g + 1)
                    nc.gpsimd.tensor_tensor(wlo[s][:], raw[s][:], whi[s][:].bitcast(F32),
                                            ALU.subtract).then_inc(S["w_ready"], 1)

                def update_odd(k):
                    for c in range(1, KC, 2):
                        pool.wait_ge(S["scaled"], KC * k + c + 1)
                        nc.gpsimd.tensor_tensor(x[:, c, :], x[:, c, :], ys[:, c, :], ALU.add).then_inc(S["xr_odd"], 1)

                def rest_odd(k):
                    for c in range(1, KC, 2):
                        pool.wait_ge(S["h_hi"], KC * (k // 2) + c + 1)
                        nc.gpsimd.tensor_tensor(hl[:, c, :], ys[:, c, :], hh[:, c, :].bitcast(F32),
                                                ALU.subtract).then_inc(S["h_odd"], 1)

                rest_odd(0)
                rest_of(1, 1)
                def forget(a):
                    pool.wait_ge(S["f_inv"], a + 1)
                    f = proj[:, B_F + a, :]
                    nc.gpsimd.tensor_scalar(f, f, lbc[:, 1, a:a + 1], lbc[:, 0, a:a + 1], ALU.mult, ALU.add)\
                        .then_inc(S["k_up"], 1)
                    pool.wait_ge(S["k_up"], 4 * a + 1)
                    nc.gpsimd.tensor_scalar(f, f, MIN_FORGET, None, ALU.max).then_inc(S["k_up"], 3)

                rest_of(2, 0)
                forget(0)
                rest_of(3, 1)
                forget(1)
                forget(2)
                rest_of(4, 0)
                forget(3)
                rest_of(5, 1)
                rest(G_LV // 2, G_LV // 2 + 1)
                rest_of(G_LV + 2, 0)

                tot = [proj[:, B_F:B_F + HR, :], f2[:], f4[:]] + [f[:] for f in f_small]
                for lv in range(1, LEVELS):
                    if lv < LEVELS - 1:
                        rest_of(G_LV + 2 + lv, lv % 2)
                    h = 1 << (lv - 1)
                    wd = TT if h <= 4 else TP
                    for a in range(HR):
                        pool.wait_ge(S["lv"], HR * lv + a + 1)
                        if lv > 1:
                            pool.wait_ge(S["k_up"], 2 * (HR * lv + a + 1))
                        f = tot[lv - 1][:, a, 0:wd // h].rearrange("p (n two) -> p n two", two=2)
                        keys = kb[:, a, 0:wd].rearrange("p (n two h) -> p n two h", two=2, h=h)
                        n = wd // (2 * h)
                        nc.gpsimd.tensor_tensor(keys[:, :, 0, :], keys[:, :, 0, :],
                                                f[:, :, 1].unsqueeze(2).broadcast_to([P, n, h]),
                                                ALU.mult).then_inc(S["k_up"], 1)
                        nc.gpsimd.tensor_tensor(tot[lv][:, a, 0:n], f[:, :, 0], f[:, :, 1], ALU.mult).then_inc(S["k_up"], 1)

                for a in range(HR):
                    if a >= 2:
                        pool.wait_ge(S["su_done"], a - 1)
                    nc.gpsimd.tensor_tensor(v_exp[a % 2][0:TS],
                                            vt[0:TS, CH, a * P:a * P + P].unsqueeze(1).broadcast_to([TS, NB, P]),
                                            seq_mask[0:TS].unsqueeze(2).broadcast_to([TS, NB, P]),
                                            ALU.mult).then_inc(S["v_wide"], 1)
                    if a == 1:
                        rest_of(G_LV + 1 + LEVELS, 1)

                pool.wait_ge(S["su_done"], HR)
                for a in range(HR):
                    pool.wait_ge(S["r_hi"], a + 1)
                    nc.gpsimd.tensor_tensor(hl[:, a, 0:TP], o_sq[:, a, 0:TP], hh[:, a, 0:TP].bitcast(F32),
                                            ALU.subtract).then_inc(S["r_lo"], 1)
                pool.wait_ge(S["r_hi"], HR + 1)
                nc.gpsimd.tensor_tensor(hl[:, 0:HR, TP:TT], rs[:].rearrange("p (a t) -> p a t", a=HR),
                                        hh[:, 0:HR, TP:TT].bitcast(F32), ALU.subtract).then_inc(S["r_lo"], 1)
                for a in range(HP):
                    if a == HP - 1:
                        pool.wait_ge(S["n_hi"], 1)
                        nc.gpsimd.tensor_tensor(hl[:, HR:HR + HP, TP:TT], t3[:, 0:HP * TS].rearrange("p (a t) -> p a t", a=HP),
                                                hh[:, HR:HR + HP, TP:TT].bitcast(F32), ALU.subtract).then_inc(S["a_lo"], 1)
                    pool.wait_ge(S["a_hi"], a + 1)
                    nc.gpsimd.tensor_tensor(hl[:, HR + a, 0:TP], t3[:, 0:TP], hh[:, HR + a, 0:TP].bitcast(F32),
                                            ALU.subtract).then_inc(S["a_lo"], 1)

                rest(G_IN // 2 + 1, (G_IN + G_OUT) // 2 + 1)
                update_odd(1)
                rest_odd(2)
                rest((G_IN + G_OUT) // 2 + 1, G_ALL // 2)
                pool.wait_ge(hi_ahead, l + 2)
                nc.gpsimd.tensor_tensor(wlo[0][:], raw[0][:], whi[0][:].bitcast(F32), ALU.subtract).then_inc(lo_ahead, 1)
                update_odd(3)

            @block.scalar
            def _(act):

                def high(g, s, first=False):
                    if first:
                        act.wait_ge(w_ahead[s], 16 * l + 16)
                    else:
                        act.wait_ge(S[f"w_in{s}"], 8 * (g - s))
                        act.wait_ge(S["blk"], 2 * g - 2)
                    nc.scalar.activation(whi[s][:], raw[s][:], ACT.Copy).then_inc(S["w_hi"], 1)

                def square(k, src, c):
                    nc.scalar.activation(sqs[:, c, :], src[:, c, :], ACT.Square).then_inc(S["sq"], 1)

                def norm_root(k):
                    act.wait_ge(S["ms"], k + 1)
                    nc.scalar.activation(root[:, 0:CH], ps[:, 4:8, 0], ACT.Sqrt, bias=eps[:], scale=1.0 / D)
                    last = ps[0:TS, 4, 1:2] if k % 2 else ps[0:TS, 3, 0:1]
                    nc.scalar.activation(root[0:TS, CH:CH + 1], last, ACT.Sqrt, bias=eps[0:TS],
                                         scale=1.0 / D).then_inc(S["root"], 1)

                def h_high(k):
                    for c in range(KC):
                        act.wait_ge(S["scaled"], KC * k + c + 1)
                        nc.scalar.activation(hh[:, c, :], ys[:, c, :], ACT.Copy).then_inc(S["h_hi"], 1)

                act.dma_start(prm[:], par[bass.ds(l, 1)].rearrange("o p n -> p (o n)")).then_inc(S["prm_in"], 16)
                norm_root(0)
                high(1, 1, True)
                h_high(0)

                def load_sampled_bias(b, h):
                    rows = slice(64 * b + TB * h, 64 * b + TB * h + TB)
                    act.dma_start(ts_cache[rows, :], bass.AP(rel_scr, h * NREL + 255, [[HA * NREL - 1, TB], [1, PAST]]))\
                        .then_inc(S["ts_in"], 16)
                    own_keys = ts_new[rows, :].rearrange("p (pair n) -> p pair n", pair=HP)[:, :, TB * b:TB * b + TB]
                    act.dma_start(own_keys, bass.AP(rel_scr, h * NREL + 511, [[HA * NREL - 1, TB], [0, HP], [1, TB]]))\
                        .then_inc(S["ts_in"], 16)

                def gate_exp(a):
                    if a >= 2:
                        act.wait_ge(S["g_gated"], a - 1)
                    nc.scalar.activation(g_tmp[a % 2][:], proj[:, B_G + a, :], ACT.Exp, scale=-1.0).then_inc(S["e_g"], 1)

                for b in range(BLK_OUT):
                    if b % 2:
                        high(b // 2 + 2, b // 2 % 2)
                    if 8 <= b < 8 + 2 * HA:
                        if b == 8:
                            act.wait_ge(c_tab, 16)
                        load_sampled_bias((b - 8) // HA, b % HA)
                    made = MADE[b]
                    if B_F <= made < B_F + HR:
                        act.wait_ge(S["free"], 2 + b + 1)
                        nc.scalar.activation(kb[:, made - B_F, :], proj[:, made, :], ACT.Exp, scale=-1.0).then_inc(S["e_f"], 1)
                    elif B_Q <= made < B_Q + HR:
                        act.wait_ge(S["free"], 2 + b + 1)
                        nc.scalar.activation(q_tmp[:, made - B_Q, :], proj[:, made, :], ACT.Exp, scale=-1.0).then_inc(S["e_q"], 1)
                    elif B_G <= made < B_G + HR:
                        a = made - B_G
                        act.wait_ge(S["free"], 2 + b + 1)
                        if a < 2:
                            gate_exp(a)
                    elif made == B_I + HR - 1:
                        for t in range(CH + 1):
                            rows = P if t < CH else TS
                            act.wait_ge(S["v_t"], t + 1)
                            nc.scalar.activation(vt[0:rows, t, :], ps[0:rows, 4 + t % 4, :], ACT.Copy).then_inc(S["v_there"], 1)
                act.wait_ge(S["free"], 2 + BLK_OUT)
                act.dma_start(kT_o[bass.ds(l, 1)].rearrange("o p j t -> p (o j) t"),
                              proj[:, B_K:B_K + HP, :]).then_inc(S["k_out"], 16)

                def load_state(a):
                    act.dma_start(s_in[a][:], s0[bass.ds(l * HR + a, 1)].rearrange("o p b v -> p (o b) v"))\
                        .then_inc(S[f"s0_in{a}"], 16)

                load_state(0)
                load_state(1)
                for a in range(HR):
                    act.wait_ge(S["k_t"], a + 1)
                    nc.scalar.activation(kt[:, a, :], ps[:, 4 + a, :], ACT.Copy).then_inc(S["k_there"], 1)
                act.wait_ge(S["k_t"], HR + 1)
                nc.scalar.activation(kts[0:TS, :], ps[0:TS, 0, :], ACT.Copy).then_inc(S["k_there"], 1)
                gate_exp(2)
                gate_exp(3)
                act.wait_ge(S["u_done"], HR)
                load_state(2)
                load_state(3)
                act.wait_ge(S["st_done"], HR)
                act.dma_start(sp_o[bass.ds(l, 1)].rearrange("o p h v -> p (o h) v"),
                              states[:, :, CH - 1, :]).then_inc(S["st_out"], 16)
                for a in range(HR):
                    act.wait_ge(S["o_done"], a + 1)
                    nc.scalar.activation(o_raw[:, a, 0:TP], ps[:, 4 + a, :], ACT.Copy).then_inc(S["o_there"], 1)
                act.wait_ge(S["o_there"], HR)
                for a in range(HR):
                    nc.scalar.activation(o_sq[:, a, 0:TP], o_raw[:, a, 0:TP], ACT.Square).then_inc(S["r_sq"], 1)

                def rec_high(a):
                    act.wait_ge(S["r_scaled"], a + 1)
                    nc.scalar.activation(hh[:, a, 0:TP], o_sq[:, a, 0:TP], ACT.Copy).then_inc(S["r_hi"], 1)

                for a in range(HR):
                    if a == 0:
                        act.wait_ge(S["r_ms"], 1)
                        nc.scalar.activation(root[:, 0:HR * CH], ps[:, 4, 0:HR * CH], ACT.Sqrt, bias=eps[:],
                                             scale=1.0 / P).then_inc(S["r_root"], 1)
                    act.wait_ge(S["s_new"], a + 1)
                    act.dma_start(ss_o[bass.ds(l * HR + a, 1)].rearrange("o p b v -> p (o b) v"),
                                  s_in[a][:]).then_inc(S["s_out"], 16)
                    if a == 1:
                        act.wait_ge(S["st_out"], 16)
                    if a:
                        rec_high(a - 1)
                nc.scalar.activation(o_raw[:, :, TP:TT], ps[:, 0, 0:HR * TS].rearrange("p (a t) -> p a t", a=HR),
                                     ACT.Copy).then_inc(S["o_there"], 1)
                act.wait_ge(S["os_set"], 1)
                nc.scalar.activation(rs[:].rearrange("p (a t) -> p a t", a=HR), o_raw[:, :, TP:TT],
                                     ACT.Square).then_inc(S["r_sq"], 1)
                rec_high(HR - 1)
                act.wait_ge(S["s_out"], 16 * HR)
                act.dma_start(bias[0][:], bass.AP(rel_scr, 127, [[HA * NREL - 1, P], [NREL, HP], [1, TP]])).then_inc(S["b_in0"], 16)

                def rec_s(k):
                    if k == 0:
                        act.wait_ge(S["r_ms"], 2)
                        nc.scalar.activation(root[0:TS, 0:HR], ps[0:TS, 7, 0:HR], ACT.Sqrt, bias=eps[0:TS],
                                             scale=1.0 / P).then_inc(S["r_root"], 1)
                        load_k(0)
                        load_v(0)
                        load_v(1)
                    else:
                        act.wait_ge(S["rs_mul"], 3)
                        nc.scalar.activation(hh[:, 0:HR, TP:TT], rs[:].rearrange("p (a t) -> p a t", a=HR),
                                             ACT.Copy).then_inc(S["r_hi"], 1)
                        act.dma_start(bias[1][:], bass.AP(rel_scr, HP * NREL + 127, [[HA * NREL - 1, P], [NREL, HP], [1, TP]]))\
                            .then_inc(S["b_in1"], 16)
                        act.wait_ge(S["r_lo"], HR)
                        load_k(1)

                def att(a, k):
                    if k == 0:
                        if a:
                            att_high(a - 1)
                        act.wait_ge(S["a_ms"], a + 1)
                        nc.scalar.activation(root[:, 0:2 * CH], ps[:, 7, 0:2 * CH], ACT.Sqrt, bias=eps[:],
                                             scale=1.0 / DH).then_inc(S["a_root"], 1)

                def att_high(a):
                    act.wait_ge(S["a_scaled"], a + 1)
                    nc.scalar.activation(hh[:, HR + a, 0:TP], t3[:, 0:TP], ACT.Copy).then_inc(S["a_hi"], 1)

                def sam_norm(k):
                    if k == 0:
                        att_high(HP - 2)
                        act.wait_ge(S["so_there"], HP)
                        act.wait_ge(S["a_ms"], HP - 1)
                        nc.scalar.activation(t1[:, 0:HP * TS].rearrange("p (a t) -> p a t", a=HP), ao[:, :, TP:TT],
                                             ACT.Square).then_inc(S["n_sq"], 1)
                        act.wait_ge(S["n_ms"], 1)
                        nc.scalar.activation(root[0:TS, 2 * CH:2 * CH + 2 * HP], ps[0:TS, 7, 0:2 * HP], ACT.Sqrt,
                                             bias=eps[0:TS], scale=1.0 / DH).then_inc(S["n_root"], 1)

                def square_pair(a):
                    if a:
                        act.wait_ge(S["a_ms"], a)
                    nc.scalar.activation(t1[:, 0:TP], ao[:, a, 0:TP], ACT.Square).then_inc(S["a_sq"], 1)

                def sam(p2, k):
                    if k == 0:
                        act.wait_ge(S["ss_max"], 4 * (p2 + 1))
                        nc.scalar.activation(ps_s[:], ps_s[:], ACT.Exp, bias=mx[:, 2, 1:2], scale=0.125,
                                             accum_out=mx[:, 2, 2:3]).then_inc(S["sp_exp"], 1)
                        if p2 + 1 < HP:
                            load_k(2 * p2 + 2)
                            load_k(2 * p2 + 3)
                    if k == 1:
                        act.wait_ge(S["sp_t"], p2 + 1)
                        nc.scalar.activation(pts[:, 0:2 * P], ps[:, 7, 0:2 * P], ACT.Copy).then_inc(S["spt_there"], 1)
                        nc.scalar.activation(pts[0:TS, 2 * P:3 * P], ps[0:TS, 7, 2 * P:3 * P], ACT.Copy).then_inc(S["spt_there"], 1)
                    if k == 3:
                        act.wait_ge(S["sel_done"], p2 + 1)
                        nc.scalar.activation(ao[:, :, TP + 2 * TB * p2:TP + 2 * TB * (p2 + 1)],
                                             ps[:, 7, 0:HP * 2 * TB].rearrange("p (a t) -> p a t", a=HP),
                                             ACT.Copy).then_inc(S["so_there"], 1)
                        if p2 + 1 < HP:
                            load_v(2 * p2 + 2)
                            load_v(2 * p2 + 3)

                steps = {"rec_s": rec_s, "att": att, "sam": sam, "sam_norm": sam_norm}

                def beside(h, place_):
                    if (h, place_) in BESIDE:
                        name, *which = BESIDE[h, place_]
                        steps[name](*which)

                def load_k(b):
                    s = b % 2
                    act.dma_start(kc[s][:], kcT[bass.ds(l * NB + b, 1)].rearrange("o p j n -> p (o j) n")).then_inc(S[f"kc_in{s}"], 16)

                def load_v(b):
                    s = b % 2
                    act.dma_start(vcs[s][:], vc[bass.ds(l * NB + b, 1)].rearrange("o p j n -> p (o j) n")).then_inc(S[f"vc_in{s}"], 16)

                for t in range(CH + 1):
                    rows = P if t < CH else TS
                    act.wait_ge(S["va_t"], t + 1)
                    nc.scalar.activation(va[0:rows, t, :], ps[0:rows, (2, 3, 0, 1, 2)[t], :], ACT.Copy).then_inc(S["va_there"], 1)
                act.wait_ge(S["va_there"], CH + 1)
                act.dma_start(v_o[bass.ds(l, 1), 0:TP, :].rearrange("o (t p) n -> p (o t) n", p=P),
                              va[:, 0:CH, :]).then_inc(S["v_out0"], 16)
                act.dma_start(v_o[bass.ds(l, 1), TP:TT, :].rearrange("o p n -> p (o n)"),
                              va[0:TS, CH, :]).then_inc(S["v_out1"], 16)
                rec_s(0)
                for h in range(HA + 2):
                    if h < HA:
                        pr, m = prob[h % 2], mx[:, h % 2, :]
                        act.wait_ge(S["s_max"], (CH + 1) * (h + 1))
                        for i in range(CH):
                            nc.scalar.activation(pr[:, tri[i]:tri[i + 1]], pr[:, tri[i]:tri[i + 1]], ACT.Exp,
                                                 bias=m[:, 4 + i:5 + i], scale=0.125,
                                                 accum_out=m[:, 8 + i:9 + i]).then_inc(S["p_exp"], 1)
                    beside(h, 0)
                    if 0 < h <= HA:
                        g = h - 1
                        if g >= 2:
                            act.wait_ge(S["pv_done"], g - 1)
                        for n, (bank, j0, j1) in enumerate(((3, 0, 1), (4, 1, 2), (5, 2, 4))):
                            act.wait_ge(S["p_t"], 3 * g + n + 1)
                            width = (trj + [tri[CH]])[j1] - trj[j0]
                            nc.scalar.activation(pt[g % 2][:, trj[j0]:trj[j0] + width], ps[:, bank, 0:width],
                                                 ACT.Copy).then_inc(S["pt_there"], 1)
                    beside(h, 1)
                    if h > 1 and h % 2:
                        act.wait_ge(S["pv_done"], h - 1)
                        nc.scalar.activation(ao[:, (h - 3) // 2, 0:TP], ps[:, 6, :], ACT.Copy).then_inc(S["ao_there"], 1)
                        if h < HA + 1:
                            act.wait_ge(S["ao_there"], (h - 1) // 2)
                            square_pair((h - 3) // 2)
                    beside(h, 2)
                beside(HA + 2, 0)
                beside(HA + 2, 1)
                act.wait_ge(S["ao_there"], HP)
                act.wait_ge(S["n_ms"], 1)
                square_pair(HP - 1)
                act.wait_ge(S["n_scaled"], 1)
                nc.scalar.activation(hh[:, HR:HR + HP, TP:TT], t3[:, 0:HP * TS].rearrange("p (a t) -> p a t", a=HP),
                                     ACT.Copy).then_inc(S["n_hi"], 1)
                act.wait_ge(S["a_ms"], HP)
                nc.scalar.activation(root[:, 0:2 * CH], ps[:, 7, 0:2 * CH], ACT.Sqrt, bias=eps[:],
                                     scale=1.0 / DH).then_inc(S["a_root"], 1)
                att_high(HP - 1)

                act.wait_ge(S["k_out"], 16)
                act.wait_ge(S["v_out0"], 16)
                act.wait_ge(S["v_out1"], 16)
                for g in range(G_OUT):
                    for c in range(2 * g, 2 * g + 2):
                        act.wait_ge(S["free"], 2 + BLK_OUT + c + 1)
                        square(1, acc, c)
                    if g < G_OUT - 1:
                        high(G_IN + 2 + g, g % 2)
                norm_root(1)
                high(G_IN + 1 + G_OUT, 1)
                for c in range(KC):
                    act.wait_ge(S["xr_odd" if c % 2 else "xr"], c // 2 + 1)
                    square(2, x, c)
                norm_root(2)
                h_high(2)
                with act.Fori((G_IN + G_OUT) // 2 + 1, G_ALL // 2 - 1) as i:
                    for s in range(2):
                        high(2 * i + s, s)
                high(G_ALL - 2, 0)
                for c in range(KC):
                    if c == 2:
                        high(G_ALL - 1, 1)
                    if c == KC - 2:
                        act.wait_ge(w_ahead[0], 16 * l + 32)
                        act.wait_ge(S["blk"], 2 * G_ALL - 2)
                        nc.scalar.activation(whi[0][:], raw[0][:], ACT.Copy).then_inc(hi_ahead, 1)
                    act.wait_ge(S["free"], 2 + 2 * (G_ALL - G_DOWN) + c + 1)
                    square(3, acc, c)
                norm_root(3)
                for c in range(KC):
                    act.wait_ge(S["xr_odd" if c % 2 else "xr"], KC // 2 + c // 2 + 1)
                    nc.scalar.activation(sqs[:, c, :], x[:, c, :], ACT.Square)
                for out, n in (("st_out", 16), ("v_out0", 16), ("v_out1", 16), ("s_out", 16 * HR)):
                    act.wait_ge(S[out], n)

            @block.tensor
            def _(pe):
                def group(g, s, src_hi=hh, src_lo=hl, ready=None):
                    pe.wait_ge(S["w_ready"], g + 1)
                    for m in range(2):
                        cols = slice(m * P, m * P + P)
                        pe.wait_ge(S["free"], 2 * g + (m + 1))
                        for c in range(KC):
                            if ready and s == 0 and m == 0:
                                name, value = ready(c)
                                pe.wait_ge(S[name], value)
                            for n, (wt, act_) in enumerate(((wlo, src_hi), (whi, src_lo), (whi, src_hi))):
                                for half in range(2):
                                    last = pe.matmul(ps[:, 2 * m + half, 0:HT], wt[s][:, c, cols],
                                                     act_[:, c, half * HT:half * HT + HT],
                                                     start=(c == 0 and n == 0), stop=(c == KC - 1 and n == 2))
                        last.then_inc(S["blk"], 1)

                def gemm(first_group, groups, src_hi, src_lo, ready):
                    with pe.Fori(0, groups // 2) as i:
                        for s in range(2):
                            group(2 * i + (first_group + s), s, src_hi, src_lo, ready)

                def tiles(blk):
                    return [(P if t < CH else TS, blk[:, t * P:t * P + (P if t < CH else TS)]) for t in range(CH + 1)]

                def norm_sum(k):
                    if k == 2:
                        blocks = [(sqs[:, c, :], "sq", KC * k + c + 1) for c in range(KC // 2)]
                        blocks += [(sqs[:, KC // 2, :], "quad", KC // 2 - 1)]
                    else:
                        blocks = [(ssq, "ssq", (KC - 2) * ((k + 3) // 2)), (sqs[:, KC - 1, :], "sq", KC * (k + 1))]
                    for n, (blk, name, value) in enumerate(blocks):
                        pe.wait_ge(S[name], value)
                        for t, (rows, cols) in enumerate(tiles(blk)):
                            if t < CH:
                                out = ps[:, 4 + t, 0:1]
                            elif k % 2 == 0:
                                out = ps[0:TS, 3, 0:1]
                            else:
                                continue
                            last = pe.matmul(out, cols, ones[:, 0:1], start=(n == 0), stop=(n == len(blocks) - 1))
                    if k % 2:
                        for n, (blk, _, _) in enumerate(blocks):
                            last = pe.matmul(ps[0:TS, 4, 1:2], tiles(blk)[CH][1], ones[:, 0:1], start=(n == 0), stop=(n == 1))
                    last.then_inc(S["ms"], 1)
                    pe.wait_ge(S["inv"], k + 1)
                    bank = 0 if k % 2 else 6
                    for t in range(CH):
                        pe.matmul(ps[:, bank, t * P:t * P + P], inv[:, t:t + 1].broadcast_to([P, P]), ident, start=True, stop=True)
                    pe.matmul(ps[:, bank + 1, 0:TS], inv[0:TS, CH:CH + 1].broadcast_to([TS, P]), ident[0:TS, 0:TS],
                              start=True, stop=True).then_inc(S["spread"], 1)

                def normed(k):
                    return lambda c: ("h_odd" if c % 2 else "h_even", KC // 2 * (k // 2) + c // 2 + 1)

                norm_sum(0)
                def level(lv, sampled):
                    for a in range(HR):
                        bank = 4 + a % 3
                        pe.wait_ge(S["q_up"], HR * lv + (a + 1))
                        pe.wait_ge(S["k_up"], 2 * HR * lv + (2 * a + 2))
                        if a == HR - 1:
                            pe.wait_ge(S["sc_set"], HR * lv + (1 + HR))
                        else:
                            pe.wait_ge(S["sc_set"], HR * lv + HR)
                        for c in range(CH):
                            last = pe.matmul(ps[:, bank, c * P:c * P + P], kb[:, a, c * P:c * P + P],
                                             proj[:, B_Q + a, c * P:c * P + P], start=True, stop=True)
                        if sampled:
                            if a == 0:
                                pe.wait_ge(S["scs_set"], lv + 1)
                            last = pe.matmul(ps[0:TS, 7, a * TS:a * TS + TS], kb[:, a, TP:TT],
                                             proj[:, B_Q + a, TP:TT], start=True, stop=True)
                        last.then_inc(S["lv"], 1)

                gemm(0, G_LV, hh, hl, normed(0))
                pe.wait_ge(S["free"], 2 + 2 * G_LV)
                for t in range(CH + 1):
                    cols = P if t < CH else TS
                    if t == CH:
                        pe.wait_ge(S["v_there"], 1)
                    for c in range(HR):
                        last = pe.transpose(ps[0:cols, 4 + t % 4, c * P:c * P + P], proj[:, B_I + c, t * P:t * P + cols], ident)
                    last.then_inc(S["v_t"], 1)
                for first, last_lv in ((0, S_LEVELS), (S_LEVELS, LEVELS)):
                    with pe.Fori(first // 2, last_lv // 2) as i:
                        pe.wait_ge(S["v_there"], CH + 1)
                        for s in range(2):
                            group(2 * i + (G_LV + s), s)
                            level(2 * i + s, last_lv == S_LEVELS)
                pe.wait_ge(S["scs_set"], S_LEVELS + 1)
                for a in range(HR):
                    pe.wait_ge(S["k_up"], 2 * (HR * LEVELS + a + 1))
                    pe.wait_ge(S["sc_set"], HR * LEVELS + HR)
                    for c in range(CH):
                        last = pe.transpose(ps[:, 4 + a, c * P:c * P + P], kb[:, a, c * P:c * P + P], ident)
                    last.then_inc(S["k_t"], 1)
                for a in range(HR):
                    last = pe.transpose(ps[0:TS, 0, a * P:a * P + P], kb[:, a, TP:TT], ident)
                last.then_inc(S["k_t"], 1)
                for a in range(HR):
                    pe.wait_ge(S["k_there"], (a + 1) if a < 3 else HR + 1)
                    for c in range(CH):
                        last = pe.matmul(ps[:, (a + 1) % 4, c * P:c * P + P], kt[:, a, c * P:c * P + P],
                                         vt[:, c, a * P:a * P + P], start=True, stop=True)
                    last.then_inc(S["u_done"], 1)
                for a in range(HR):
                    pe.wait_ge(S["st_done"], a + 1)
                    pe.wait_ge(S["q_up"], HR * LEVELS + a + 1)
                    for c in range(CH):
                        cs = slice(c * P, c * P + P)
                        last = pe.matmul(ps[:, 4 + a, cs], vt[:, c, a * P:a * P + P], sc[:, a, cs], start=True, stop=(c == 0))
                        if c:
                            last = pe.matmul(ps[:, 4 + a, cs], states[:, a, c - 1, :], proj[:, B_Q + a, cs], start=False, stop=True)
                    last.then_inc(S["o_done"], 1)
                def rec_sums():
                    for a in range(HR):
                        for t in range(CH):
                            last = pe.matmul(ps[:, 4, a * CH + t:a * CH + t + 1], tiles(o_sq[:, a, :])[t][1], ones[:, 0:1],
                                             start=True, stop=True)
                    last.then_inc(S["r_ms"], 1)

                def rec_spread(a):
                    if a == 0:
                        pe.wait_ge(S["r_inv"], 1)
                    if a >= 2:
                        pe.wait_ge(S["r_scaled"], a - 1)
                    for t in range(CH):
                        c = a * CH + t
                        last = pe.matmul(ps[:, 5 - a % 2, t * P:t * P + P], inv[:, c:c + 1].broadcast_to([P, P]), ident,
                                         start=True, stop=True)
                    last.then_inc(S["r_spread"], 1)

                for a in range(HR):
                    pe.wait_ge(S[f"s0_in{a}"], 16)
                    pe.matmul(ps[:, 0, a * TS:a * TS + TS], vt[0:TS, CH, a * P:a * P + P], scs[0:TS, a, :],
                              start=True, stop=True)
                    for b in range(NB):
                        o0 = a * TS + b * TB
                        pe.matmul(ps[:, 1, o0:o0 + TB], s_in[a][:, b, :],
                                  proj[:, B_Q + a, TP + b * TB:TP + b * TB + TB], start=True, stop=True)
                    pe.wait_ge(S["v_wide"], a + 1)
                    if a >= 2:
                        pe.wait_ge(S["s_new"], a - 1)
                    elif a:
                        pe.wait_ge(S["o_there"], HR)
                    for half in range(2):
                        last = pe.matmul(ps[:, 2 + 4 * (a % 2) + half, :], kts[0:TS, a * P:a * P + P],
                                         v_exp[a % 2][0:TS, 4 * half:4 * half + 4, :], start=True, stop=True)
                    last.then_inc(S["su_done"], 1)
                    if a == 0:
                        pe.wait_ge(S["o_there"], HR)
                        pe.wait_ge(S["r_sq"], HR)
                        rec_sums()
                    else:
                        rec_spread(a - 1)
                va_bank = [2, 3, 0, 1, 2]
                for t in range(CH + 1):
                    cols = P if t < CH else TS
                    if t == 0:
                        pe.wait_ge(S["s_new"], HR - 1)
                    if t == 2:
                        rec_spread(HR - 1)
                        pe.wait_ge(S["os_set"], 1)
                    if t == CH:
                        pe.wait_ge(S["va_there"], 1)
                    for c in range(HP):
                        last = pe.transpose(ps[0:cols, va_bank[t], c * P:c * P + P], proj[:, B_V + c, t * P:t * P + cols], ident)
                    last.then_inc(S["va_t"], 1)

                def rec_s(k):
                    free_7()
                    if k == 0:
                        pe.wait_ge(S["r_sq"], HR + 1)
                        for a in range(HR):
                            last = pe.matmul(ps[0:TS, 7, a:a + 1], rs[:, a * TS:a * TS + TS], ones[:, 0:1],
                                             start=True, stop=True)
                        last.then_inc(S["r_ms"], 1)
                        bank_7[0] = ("r_root", 2)
                    else:
                        pe.wait_ge(S["r_inv"], 2)
                        for a in range(HR):
                            last = pe.matmul(ps[:, 7, a * TS:a * TS + TS], inv[0:TS, a:a + 1].broadcast_to([TS, P]),
                                             ident[0:TS, 0:TS], start=True, stop=True)
                        last.then_inc(S["r_spread"], 1)
                        bank_7[0] = ("rs_mul", 1)

                def att(a, k):
                    free_7()
                    if k == 0:
                        pe.wait_ge(S["a_sq"], a + 1)
                        for t in range(CH):
                            last = pe.matmul(ps[:, 7, 2 * t:2 * t + 2], t1[:, t * P:t * P + P], half_ones[:, 0:P:DH],
                                             start=True, stop=True)
                        last.then_inc(S["a_ms"], 1)
                        bank_7[0] = ("a_root", a + 1)
                    else:
                        pe.wait_ge(S["a_inv"], a + 1)
                        for t in range(CH):
                            for s in range(2):
                                last = pe.matmul(ps[DH * s:DH * s + DH, 7, t * P:t * P + P],
                                                 inv[:, 2 * t + s:2 * t + s + 1].broadcast_to([P, DH]), ident,
                                                 start=True, stop=True)
                        last.then_inc(S["a_spread"], 1)
                        bank_7[0] = ("a_scaled", a + 1)

                def sam_norm(k):
                    free_7()
                    if k == 0:
                        pe.wait_ge(S["n_sq"], 1)
                        for a in range(HP):
                            last = pe.matmul(ps[0:TS, 7, 2 * a:2 * a + 2], t1[:, a * TS:a * TS + TS], half_ones[:, 0:P:DH],
                                             start=True, stop=True)
                        last.then_inc(S["n_ms"], 1)
                        bank_7[0] = ("n_root", 1)
                    else:
                        pe.wait_ge(S["n_inv"], 1)
                        for a in range(HP):
                            for s in range(2):
                                c = 2 * CH + 2 * a + s
                                last = pe.matmul(ps[DH * s:DH * s + DH, 7, a * TS:a * TS + TS],
                                                 inv[0:TS, c:c + 1].broadcast_to([TS, DH]), ident[0:TS, 0:TS],
                                                 start=True, stop=True)
                        last.then_inc(S["n_spread"], 1)
                        bank_7[0] = ("n_scaled", 1)

                def sam(p2, k):
                    free_7()
                    if k == 0:
                        for s in range(2):
                            pe.wait_ge(S[f"kc_in{s}"], 16 * (p2 + 1))
                            r = slice(64 * s, 64 * s + 64)
                            for j in range(HP):
                                q0 = (2 * p2 + s) * 64
                                pe.matmul(ps[r, 7, 0:PAST], qbig[:, j, q0:q0 + 64], kc[s][:, j, :],
                                          start=(j == 0), stop=(j == HP - 1))
                        for j in range(HP):
                            last = pe.matmul(ps[:, 7, PAST:PAST + TS], qbig[:, j, p2 * P:p2 * P + P], proj[:, B_K + j, TP:TT],
                                             start=(j == 0), stop=(j == HP - 1))
                        last.then_inc(S["ss_done"], 1)
                        bank_7[0] = ("ss_max", 4 * p2 + 2)
                    if k == 1:
                        pe.wait_ge(S["sp_norm"], p2 + 1)
                        for k2 in range(2):
                            pe.transpose(ps[:, 7, k2 * P:k2 * P + P], ps_s[:, k2 * P:k2 * P + P], ident)
                        pe.transpose(ps[0:TS, 7, 2 * P:3 * P], ps_s[:, PAST:PAST + TS], ident).then_inc(S["sp_t"], 1)
                        bank_7[0] = ("spt_there", 2 * (p2 + 1))
                    if k == 2:
                        for s in range(2):
                            pe.wait_ge(S[f"vc_in{s}"], 16 * (p2 + 1))
                            for k2 in range(2):
                                pe.matmul(ps[64 * s:64 * s + 64, 7, :], pts[:, k2 * P + 64 * s:k2 * P + 64 * s + 64],
                                          vcs[s][:, k2, :], start=(k2 == 0), stop=False)
                        last = pe.matmul(ps[:, 7, :], pts[0:TS, 2 * P:3 * P], va[0:TS, CH, :], start=False, stop=True)
                        last.then_inc(S["spv_done"], 1)
                        bank_7[0] = ("mo_set", p2 + 1)
                    if k == 3:
                        for c in range(HP):
                            last = pe.matmul(ps[:, 7, c * 2 * TB:(c + 1) * 2 * TB], mo[:, c * P:c * P + P], tok_sel,
                                             start=True, stop=True)
                        last.then_inc(S["sel_done"], 1)
                        bank_7[0] = ("so_there", p2 + 1)

                steps = {"rec_s": rec_s, "att": att, "sam": sam, "sam_norm": sam_norm}

                def beside(h, place_):
                    if (h, place_) in BESIDE:
                        name, *which = BESIDE[h, place_]
                        steps[name](*which)

                bank_7 = [("s_new", HR)]

                def free_7():
                    pe.wait_ge(S[bank_7[0][0]], bank_7[0][1])

                rec_s(0)
                pe.wait_ge(S["qb"], 1)
                for h in range(HA + 2):
                    if h < HA:
                        r = slice(DH * (h % 2), DH * (h % 2) + DH)
                        if h:
                            pe.wait_ge(S["s_max"], (CH + 1) * h)
                        else:
                            pe.wait_ge(S["va_there"], CH + 1)
                        for i, (bank, c0) in s_at.items():
                            last = pe.matmul(ps[:, bank, c0:c0 + (i + 1) * P], proj[r, B_QA + h // 2, i * P:i * P + P],
                                             proj[r, B_K + h // 2, 0:(i + 1) * P], start=True, stop=True)
                            if i:
                                last.then_inc(S["s_done"], 1)
                    beside(h, 0)
                    if 0 < h <= HA:
                        g = h - 1
                        pe.wait_ge(S["p_norm"], CH * (g + 1))
                        if g:
                            pe.wait_ge(S["pt_there"], 3 * g)
                        for bank, js in ((3, (0,)), (4, (1,)), (5, (2, 3))):
                            for j in js:
                                for i in range(j, CH):
                                    c0 = trj[j] - trj[js[0]] + (i - j) * P
                                    last = pe.transpose(ps[:, bank, c0:c0 + P],
                                                        prob[g % 2][:, tri[i] + j * P:tri[i] + j * P + P], ident)
                            last.then_inc(S["p_t"], 1)
                    beside(h, 1)
                    if h > 1:
                        g = h - 2
                        r = slice(DH * (g % 2), DH * (g % 2) + DH)
                        pe.wait_ge(S["pt_there"], 3 * (g + 1))
                        if g % 2 == 0 and g:
                            pe.wait_ge(S["ao_there"], g // 2)
                        for i in range(CH):
                            for j in range(i + 1):
                                c0 = trj[j] + (i - j) * P
                                last = pe.matmul(ps[r, 6, i * P:i * P + P], va[:, j, g * DH:g * DH + DH],
                                                 pt[g % 2][:, c0:c0 + P], start=(j == 0), stop=(j == i))
                        last.then_inc(S["pv_done"], 1)
                    beside(h, 2)
                beside(HA + 2, 0)
                beside(HA + 2, 1)
                att(HP - 1, 0)
                att(HP - 1, 1)

                gemm(G_IN, G_OUT, hh, hl, lambda c: ("r_lo", HR + 1) if c < HR else ("a_lo", HP if c < KC - 1 else HP + 1))
                norm_sum(1)
                norm_sum(2)
                with pe.Fori(0, NQ) as q:
                    g0 = q * (G_UP + G_DOWN) + (G_IN + G_OUT)
                    gemm(g0, G_UP, hh, hl, normed(2))
                    gemm(g0 + G_UP, G_DOWN, uh, ul, lambda c: ("u_set", q * KC + (c + 1)))
                norm_sum(3)

            @block.vector
            def _(dve):
                own = Steps(dve, S["dv"])
                V = nc.vector

                def sum_squares(k, c):
                    if c < 2:
                        return
                    n = (KC - 2) * ((k + 1) // 2)
                    dve.wait_ge(S["sq"], KC * k + c)
                    if c > 2:
                        dve.wait_ge(S["ssq"], n + c - 2)
                    V.tensor_tensor(ssq, sqs[:, 0, :] if c == 2 else ssq, sqs[:, c - 1, :], ALU.add).then_inc(S["ssq"], 1)

                def norm_apply(k, gains, post):
                    dve.wait_ge(S["root"], k + 1)
                    V.reciprocal(inv[:, 0:CH], root[:, 0:CH])
                    V.reciprocal(inv[0:TS, CH:CH + 1], root[0:TS, CH:CH + 1]).then_inc(S["inv"], 1)
                    dve.wait_ge(S["spread"], k + 1)
                    bank = 0 if k % 2 else 6
                    every = ps[:, bank:bank + 2, :].rearrange("p a b -> p (a b)")[:, 0:TT]
                    src = acc if post else x
                    for c in range(KC + 2):
                        if c < KC:
                            V.scalar_tensor_tensor(ys[:, c, :], src[:, c, :], gains[:, c:c + 1], every,
                                                   ALU.mult, ALU.mult).then_inc(S["scaled"], 1)
                        b = c - 1 if post else c - 2
                        if b < 0 or b % 2 or b >= KC:
                            continue
                        if post:
                            dve.wait_ge(S["scaled"], KC * k + b + 1)
                            V.tensor_tensor(x[:, b, :], x[:, b, :], ys[:, b, :], ALU.add).then_inc(S["xr"], 1)
                        else:
                            dve.wait_ge(S["h_hi"], KC * (k // 2) + b + 1)
                            V.tensor_tensor(hl[:, b, :], ys[:, b, :], hh[:, b, :].bitcast(F32),
                                            ALU.subtract).then_inc(S["h_even"], 1)

                def sigmoid_parts(e):
                    own(V.tensor_scalar(e, e, 1.0, None, ALU.add))
                    own.wait()
                    own(V.reciprocal(e, e))
                    own.wait()

                V.memset(mx[:, 0, 0:8], 0.0).then_inc(S["free"], 2)
                V.memset(mx[:, 1], 0.0).then_inc(S["w_hi"], 1)
                V.memset(mx[:, 0, 8:16], 0.0).then_inc(S["sq"], KC)
                V.memset(mx[:, 2], 0.0).then_inc(S["w_ready"], 1)
                own(V.tensor_copy(lbc[:, 0:1, :], lb[:, bass.ds(l, 1), :]))
                own.wait()
                own(V.tensor_scalar(lbc[:, 1, :], lbc[:, 0, :], -1.0, 1.0, ALU.mult, ALU.add))
                for c in range(2, KC):
                    sum_squares(0, c)
                dve.wait_ge(S["prm_in"], 16)
                norm_apply(0, prm[:, 0:KC], False)

                dve.wait_ge(c_row, 16)
                zf, qq, gg = (proj[:, b0:b0 + HR, :] for b0 in (B_F, B_Q, B_G))
                def gate_f(a):
                    k, f = kb[:, a, :], zf[:, a, :]
                    dve.wait_ge(S["e_f"], a + 1)
                    own(V.tensor_scalar(f, k, 1.0, None, ALU.add))
                    own.wait()
                    own(V.reciprocal(f, f))
                    own.wait()
                    V.scalar_tensor_tensor(k, k, lbc[:, 1, a:a + 1], f, ALU.mult, ALU.mult).then_inc(S["f_inv"], 1)

                def gate_q(a):
                    e = q_tmp[:, a, :]
                    dve.wait_ge(S["e_q"], a + 1)
                    own(V.tensor_scalar(e, e, 1.0, None, ALU.add))
                    own.wait()
                    own(V.reciprocal(e, e))
                    own.wait()
                    V.tensor_tensor(qq[:, a, :], qq[:, a, :], e, ALU.mult).then_inc(S["q_up"], 1)

                def gate_g(a):
                    e = g_tmp[a % 2][:]
                    dve.wait_ge(S["e_g"], a + 1)
                    own(V.tensor_scalar(e, e, 1.0, None, ALU.add))
                    own.wait()
                    own(V.reciprocal(e, e))
                    own.wait()
                    V.tensor_tensor(gg[:, a, :], gg[:, a, :], e, ALU.mult).then_inc(S["g_gated"], 1)

                def level(lv):
                    for a in range(HR):
                        dve.wait_ge(S["lv"], HR * lv + a + 1)
                        V.copy_predicated(out=sc[:, a, :].rearrange("p (c t) -> p c t", c=CH),
                                          mask=masks[:, lv, :].unsqueeze(1).broadcast_to([P, CH, P]),
                                          data=ps[:, 4 + a % 3, :].rearrange("p (c t) -> p c t", c=CH)).then_inc(S["sc_set"], 1)
                        if lv == 0:
                            V.tensor_tensor(qq[:, a, :], qq[:, a, :], zf[:, a, :], ALU.mult).then_inc(S["q_up"], 1)
                        else:
                            h = 1 << (lv - 1)
                            wd = TT if h <= 4 else TP
                            n = wd // (2 * h)
                            if lv > 1:
                                dve.wait_ge(S["k_up"], 2 * (HR * lv + a + 1))
                            f = tot[lv - 1][:, a, 0:wd // h].rearrange("p (n two) -> p n two", two=2)
                            q = qq[:, a, 0:wd].rearrange("p (n two h) -> p n two h", two=2, h=h)[:, :, 1, :]
                            V.tensor_tensor(q, q, f[:, :, 0].unsqueeze(2).broadcast_to([P, n, h]),
                                            ALU.mult).then_inc(S["q_up"], 1)
                    if lv < S_LEVELS:
                        V.copy_predicated(out=scs[0:TS], mask=masks[0:TS, lv, 0:TS].unsqueeze(1).broadcast_to([TS, HR, TS]),
                                          data=ps[0:TS, 7, 0:HR * TS].rearrange("p (a t) -> p a t", a=HR))\
                            .then_inc(S["scs_set"], 1)
                    dve.wait_ge(S["sc_set"], HR * lv + 2 * HR)
                    dve.wait_ge(S["q_up"], HR * lv + 2 * HR)
                    if lv < S_LEVELS:
                        dve.wait_ge(S["scs_set"], lv + 2)

                tot = [zf, f2[:], f4[:]] + [f[:] for f in f_small]
                for b in range(BLK_OUT):
                    made = MADE[b]
                    dve.wait_ge(S["blk"], b + 1)
                    if B_F <= made < B_F + HR:
                        V.tensor_scalar(halves(proj[:, made, :]), pair_of(b % 2), -80.0, None, ALU.max).then_inc(S["free"], 1)
                    else:
                        V.tensor_copy(halves(proj[:, made, :]), pair_of(b % 2)).then_inc(S["free"], 1)
                    if 1 <= b <= HR:
                        gate_f(b - 1)
                    elif HR < b <= 2 * HR:
                        gate_q(b - 1 - HR)
                    elif b == 2 * G_LV:
                        dve.wait_ge(S["v_t"], CH + 1)
                        V.memset(sc[:], 0.0).then_inc(S["sc_set"], HR)
                        V.memset(scs[0:TS], 0.0).then_inc(S["scs_set"], 1)
                        dve.wait_ge(S["sc_set"], HR)
                        dve.wait_ge(S["scs_set"], 1)
                        dve.wait_ge(S["q_up"], HR)
                        dve.wait_ge(S["k_up"], 4 * HR)
                    if b > 2 * G_LV and b % 2:
                        level(b // 2 - G_LV)
                    if made in (B_G + 1, B_G + 2):
                        gate_g(made - B_G - 1)
                    if b == BLK_OUT - HR - 1:
                        dve.wait_ge(S["k_up"], 2 * HR * 5)

                for j in range(HP):
                    qv = qbig[:, j, :].rearrange("p (b h t) -> p b h t", b=NB, h=HA)
                    for s in range(2):
                        r = slice(DH * s, DH * s + DH)
                        ins = V.tensor_copy(qv[r, :, 2 * j + s, :],
                                            proj[r, B_QA + j, TP:TT].rearrange("p (b t) -> p b t", b=NB))
                ins.then_inc(S["qb"], 1)
                dve.wait_ge(S["k_up"], 2 * HR * (LEVELS + 1))
                for a in range(HR):
                    dve.wait_ge(S["u_done"], a + 1)
                    bank = (a + 1) % 4
                    own(V.tensor_copy(states[:, a, 0, :], ps[:, bank, 0:P]))
                    for c in range(1, CH):
                        own.wait()
                        ins = V.scalar_tensor_tensor(states[:, a, c, :], states[:, a, c - 1, :], f_small[4][:, a, c:c + 1],
                                                     ps[:, bank, c * P:c * P + P], ALU.mult, ALU.add)
                        if c < CH - 1:
                            own(ins)
                        else:
                            ins.then_inc(S["st_done"], 1)
                rgain = prm[:, 4 * KC:4 * KC + HR]

                def rec(a):
                    dve.wait_ge(S["r_spread"], a + 1)
                    own(V.scalar_tensor_tensor(o_sq[:, a, 0:TP], o_raw[:, a, 0:TP], rgain[:, a:a + 1], ps[:, 5 - a % 2, :],
                                               ALU.mult, ALU.mult))
                    own.wait()
                    V.tensor_tensor(o_sq[:, a, 0:TP], o_sq[:, a, 0:TP], gg[:, a, 0:TP], ALU.mult).then_inc(S["r_scaled"], 1)

                gate_g(2)
                for a in range(HR):
                    s = s_in[a]
                    dve.wait_ge(S["su_done"], a + 1)
                    own(V.tensor_tensor(s[:], s[:], f_small[0][:, a, TP // TB:TT // TB].unsqueeze(2).broadcast_to([P, NB, P]),
                                        ALU.mult))
                    own.wait()
                    V.tensor_tensor(s[:].rearrange("p b v -> p (b v)"), s[:].rearrange("p b v -> p (b v)"),
                                    ps[:, 2 + 4 * (a % 2):4 + 4 * (a % 2), :].rearrange("p a b -> p (a b)"),
                                    ALU.add).then_inc(S["s_new"], 1)
                    if a == 0:
                        dve.wait_ge(S["r_root"], 1)
                        V.reciprocal(inv[:, 0:HR * CH], root[:, 0:HR * CH]).then_inc(S["r_inv"], 1)
                        gate_g(3)
                    if a:
                        rec(a - 1)
                dve.wait_ge(S["o_there"], HR + 1)
                outs = o_raw[:, :, TP:TT]
                V.tensor_tensor(outs, outs, ps[:, 1, 0:HR * TS].rearrange("p (a t) -> p a t", a=HR),
                                ALU.add).then_inc(S["os_set"], 1)
                rec(HR - 1)

                def rec_s(k):
                    if k == 0:
                        dve.wait_ge(S["r_root"], 2)
                        V.reciprocal(inv[0:TS, 0:HR], root[0:TS, 0:HR]).then_inc(S["r_inv"], 1)
                        return
                    normed_ = rs[:].rearrange("p (a t) -> p a t", a=HR)
                    dve.wait_ge(S["r_spread"], HR + 1)
                    V.tensor_tensor(normed_, outs, ps[:, 7, 0:HR * TS].rearrange("p (a t) -> p a t", a=HR),
                                    ALU.mult).then_inc(S["rs_mul"], 1)
                    dve.wait_ge(S["rs_mul"], 1)
                    V.tensor_tensor(normed_, normed_, rgain.unsqueeze(2).broadcast_to([P, HR, TS]), ALU.mult)\
                        .then_inc(S["rs_mul"], 1)
                    dve.wait_ge(S["rs_mul"], 2)
                    V.tensor_tensor(normed_, normed_, gg[:, :, TP:TT], ALU.mult).then_inc(S["rs_mul"], 1)

                gain = prm[:, 4 * KC + HR:4 * KC + HR + HP]

                def att(a, k):
                    if k == 0:
                        dve.wait_ge(S["a_root"], a + 1)
                        V.reciprocal(inv[:, 0:2 * CH], root[:, 0:2 * CH]).then_inc(S["a_inv"], 1)
                    else:
                        dve.wait_ge(S["a_spread"], a + 1)
                        if a:
                            dve.wait_ge(S["a_lo"], a if a < HP - 1 else HP)
                        V.scalar_tensor_tensor(t3[:, 0:TP], ao[:, a, 0:TP], gain[:, a:a + 1], ps[:, 7, :],
                                               ALU.mult, ALU.mult).then_inc(S["a_scaled"], 1)

                def sam_norm(k):
                    if k == 0:
                        dve.wait_ge(S["n_root"], 1)
                        c = slice(2 * CH, 2 * CH + 2 * HP)
                        V.reciprocal(inv[0:TS, c], root[0:TS, c]).then_inc(S["n_inv"], 1)
                    else:
                        dve.wait_ge(S["n_spread"], 1)
                        dve.wait_ge(S["a_lo"], HP - 1)
                        for a in range(HP):
                            cols = slice(a * TS, a * TS + TS)
                            ins = V.scalar_tensor_tensor(t3[:, cols], ao[:, a, TP:TT], gain[:, a:a + 1], ps[:, 7, cols],
                                                         ALU.mult, ALU.mult)
                        ins.then_inc(S["n_scaled"], 1)

                def sam(p2, k):
                    m = mx[:, 2, :]
                    if k == 0:
                        if p2 == 0:
                            dve.wait_ge(S["ts_in"], 16 * 4 * HA)
                            dve.wait_ge(S["rs_mul"], 3)
                        dve.wait_ge(S["ss_done"], p2 + 1)
                        V.tensor_tensor(ps_s[:, 0:PAST], ps[:, 7, 0:PAST], ts_cache[:], ALU.add).then_inc(S["ss_max"], 1)
                        V.tensor_tensor(ps_s[:, PAST:PAST + TS], ps[:, 7, PAST:PAST + TS],
                                        ts_new[:, p2 * TS:p2 * TS + TS], ALU.add).then_inc(S["ss_max"], 1)
                        dve.wait_ge(S["ss_max"], 4 * p2 + 2)
                        V.reduce_max(m[:, 0:1], ps_s[:], AX.X).then_inc(S["ss_max"], 1)
                        dve.wait_ge(S["ss_max"], 4 * p2 + 3)
                        V.tensor_scalar(m[:, 1:2], m[:, 0:1], -0.125, None, ALU.mult).then_inc(S["ss_max"], 1)
                    if k == 1:
                        dve.wait_ge(S["sp_exp"], p2 + 1)
                        own(V.reciprocal(m[:, 3:4], m[:, 2:3]))
                        own.wait()
                        V.tensor_scalar(ps_s[:], ps_s[:], m[:, 3:4], None, ALU.mult).then_inc(S["sp_norm"], 1)
                    if k == 2:
                        dve.wait_ge(S["spv_done"], p2 + 1)
                        V.tensor_tensor(mo[:].rearrange("p (h d) -> p h d", h=HA),
                                        ps[:, 7, :].rearrange("p (h d) -> p h d", h=HA),
                                        head_mask.unsqueeze(2).broadcast_to([P, HA, DH]), ALU.mult).then_inc(S["mo_set"], 1)

                steps = {"rec_s": rec_s, "att": att, "sam": sam, "sam_norm": sam_norm}

                def beside(h, place_):
                    if (h, place_) in BESIDE:
                        name, *which = BESIDE[h, place_]
                        steps[name](*which)

                rec_s(0)
                for h in range(HA + 2):
                    if 0 < h <= HA:
                        g = h - 1
                        pr, m = prob[g % 2], mx[:, g % 2, :]
                        dve.wait_ge(S["p_exp"], CH * (g + 1))
                        own(V.reciprocal(m[:, 12:16], m[:, 8:12]))
                        own.wait()
                        for i in range(CH):
                            V.tensor_scalar(pr[:, tri[i]:tri[i + 1]], pr[:, tri[i]:tri[i + 1]], m[:, 12 + i:13 + i], None,
                                            ALU.mult).then_inc(S["p_norm"], 1)
                    if h < HA:
                        pr, m = prob[h % 2], mx[:, h % 2, :]
                        if h % HP == 0:
                            dve.wait_ge(S[f"b_in{h // HP}"], 16)
                        if h == 1:
                            dve.wait_ge(S["r_lo"], HR)
                        if h >= 2:
                            dve.wait_ge(S["p_t"], 3 * (h - 1))
                        for n, (i, (bank, c0)) in enumerate(s_at.items()):
                            if n < CH - 1:
                                dve.wait_ge(S["s_done"], (CH - 1) * h + n + 1)
                            V.tensor_tensor_reduce(out=pr[:, tri[i]:tri[i + 1]], in0=ps[:, bank, c0:c0 + (i + 1) * P],
                                                   in1=bias[h // HP][:, h % HP, (CH - 1 - i) * P:TP], scale=1.0, scalar=-3.0e38,
                                                   op0=ALU.add, op1=ALU.max, accum_out=m[:, i:i + 1]).then_inc(S["s_max"], 1)
                        dve.wait_ge(S["s_max"], (CH + 1) * h + CH)
                        V.tensor_scalar(m[:, 4:8], m[:, 0:4], -0.125, None, ALU.mult).then_inc(S["s_max"], 1)
                    for place_ in range(3):
                        beside(h, place_)
                beside(HA + 2, 0)
                beside(HA + 2, 1)
                att(HP - 1, 0)
                att(HP - 1, 1)

                def leave(b, add):
                    i, k, before = b
                    dve.wait_ge(S["blk"], 4 * i + (k + 1 + before))
                    dst = acc[:, bass.ds(4 * i + k, 1), :].rearrange("p o (a t) -> p (o a) t", a=2)
                    if add:
                        V.tensor_tensor(dst, dst, pair_of(k % 2), ALU.add).then_inc(S["free"], 1)
                    else:
                        V.tensor_copy(dst, pair_of(k % 2)).then_inc(S["free"], 1)

                for c in range(KC):
                    leave((c // 4, c % 4, BLK_OUT), False)
                    sum_squares(1, c)
                norm_apply(1, prm[:, KC:2 * KC], True)
                for n in range(1, KC // 2):
                    c = KC // 2 + n
                    dve.wait_ge(S["sq"], 2 * KC + c + 1)
                    if n > 1:
                        dve.wait_ge(S["quad"], n - 1)
                    V.tensor_tensor(sqs[:, KC // 2, :], sqs[:, KC // 2, :], sqs[:, c, :], ALU.add).then_inc(S["quad"], 1)
                norm_apply(2, prm[:, 2 * KC:3 * KC], False)

                def up(q):
                    with own.loop(0, G_UP // 2, 2 * 4) as i:
                        for k in range(4):
                            b = q * BLK_Q + BLK_MLP
                            dve.wait_ge(S["blk"], 4 * i + (k + 1) + b)
                            V.tensor_scalar(halves(t1[:]), pair_of(k % 2), 0.0, None, ALU.max).then_inc(S["free"], 1)
                            dve.wait_ge(S["free"], 4 * i + (k + 3) + b)
                            own(V.tensor_tensor(t2[:], t1[:], t1[:], ALU.mult))
                            own.wait()
                            u = uh[:, bass.ds(4 * i + k, 1), :].rearrange("p o t -> p (o t)")
                            own(V.tensor_copy(u, t2[:]))
                            own.wait()
                            u2 = ul[:, bass.ds(4 * i + k, 1), :].rearrange("p o t -> p (o t)")
                            V.tensor_tensor(u2, t2[:], u.bitcast(F32), ALU.subtract).then_inc(S["u_set"], 1)
                            dve.wait_ge(S["u_set"], 4 * i + (k + 1) + q * KC)

                def down(q, add):
                    with dve.Fori(0, G_DOWN // 2) as i:
                        for k in range(4):
                            leave((i, k, q * BLK_Q + (BLK_MLP + 2 * G_UP)), add)

                up(0)
                down(0, False)
                n0 = own.n
                per = 2 * 8
                with dve.Fori(1, NQ - 1) as q:
                    own.n = n0 + (q - 1) * per
                    up(q)
                    down(q, True)
                own.n = n0 + (NQ - 2) * per
                up(NQ - 1)
                for c in range(KC):
                    leave((c // 4, c % 4, 2 * (G_ALL - G_DOWN)), True)
                    sum_squares(3, c)
                norm_apply(3, prm[:, 3 * KC:4 * KC], True)

        nc.sync.sem_clear(range(nums[0], nums[-1] + 1))
        nc.all_engine_barrier()

    y_out = sem("y_out")
    with nc.Block() as block:
        @block.sync
        def _(sp):
            sp.dma_start(yT, x[:]).then_inc(y_out, 16)
            sp.wait_ge(y_out, 16)
            for s in range(2):
                sp.wait_ge(w_ahead[s], 16 * (DEPTH + 1))
    ctx.close()


def kernel(x_prompt, x_sample, state_hgrn, cache_k, cache_v, rel_bias, lb_raw, w_in, w_out, w_up, w_down,
           g_mix_pre, g_mix_post, g_mlp_pre, g_mlp_post, g_rec_out, g_attn_out):
    import concourse.bacc as bacc
    from concourse.bass_utils import run_bass_kernel_spmd

    f = lambda a: np.asarray(a)
    L = DEPTH
    x = np.concatenate([f(x_prompt).reshape(TP, D), f(x_sample).reshape(TS, D)], 0)
    blocks = lambda m, n: m.reshape(n, P, -1).transpose(1, 0, 2)

    def groups(m):
        return m.reshape(KC, P, -1, GC).transpose(2, 1, 0, 3).reshape(-1, P, KC * GC)

    order = [1, 0, 2, 6, 5, 4, 3]
    ws = []
    for l in range(L):
        wi = f(w_in)[l]
        parts = [groups(np.concatenate([wi[:, 512 * o:512 * o + 512] for o in order], 1)), groups(f(w_out)[l])]
        for q in range(NQ):
            n = FF // NQ
            parts += [groups(f(w_up)[l][:, q * n:q * n + n]), groups(f(w_down)[l][q * n:q * n + n, :])]
        ws += parts
    cst, masks, rel = constants()
    cols = lambda g, n: f(g).reshape(L, n, P).transpose(0, 2, 1)
    ins = {
        "xT": blocks(x.T, KC),
        "w": np.concatenate(ws, 0),
        "par": np.concatenate([cols(g, KC) for g in (g_mix_pre, g_mix_post, g_mlp_pre, g_mlp_post)]
                              + [cols(g_rec_out, HR), cols(g_attn_out, HP)], 2),
        "lbr": f(lb_raw).reshape(L, HR, P).transpose(2, 0, 1),
        "relb": f(rel_bias),
        "s0": f(state_hgrn).transpose(0, 2, 3, 1, 4).reshape(L * HR, P, NB, P),
        "kcT": f(cache_k).reshape(L * NB, PAST, HP, P).transpose(0, 3, 2, 1),
        "vc": f(cache_v).reshape(L * NB, 2, P, 512).transpose(0, 2, 1, 3),
        "cst": cst, "msk": masks, "rel": rel,
    }
    ins = {k: np.ascontiguousarray(v) for k, v in ins.items()}
    outs = {"yT": (P, KC, TT), "sp": (L, P, HR, P), "kT": (L, P, HP, TT), "vo": (L, TT, 512), "ss": (L * HR, P, NB, P)}
    nc = bacc.Bacc("TRN2", target_bir_lowering=False, num_devices=1)
    i_aps = [nc.dram_tensor(k, v.shape, mybir.dt.from_np(v.dtype), kind="ExternalInput").ap() for k, v in ins.items()]
    o_aps = [nc.dram_tensor(k, s, F32, kind="ExternalOutput").ap() for k, s in outs.items()]
    scratch = nc.dram_tensor("rel_scratch", (P, HA, NREL), F32)
    build(nc, *i_aps, *o_aps, nc.dram_tensor("rel_row", (HA, NREL), F32), scratch)
    r = run_bass_kernel_spmd(nc, [ins], core_ids=[0]).results[0]
    y = r["yT"].transpose(1, 0, 2).reshape(D, TT).T
    k_new = r["kT"].transpose(0, 3, 2, 1).reshape(L, TT, HA, DH)
    v_new = r["vo"].reshape(L, TT, HA, DH)
    return (y[:TP].reshape(1, TP, D), y[TP:].reshape(NB, TB, D),
            r["sp"].transpose(0, 2, 1, 3).reshape(L, 1, HR, P, P),
            k_new[:, :TP].reshape(L, 1, TP, HA, DH), v_new[:, :TP].reshape(L, 1, TP, HA, DH),
            r["ss"].reshape(L, HR, P, NB, P).transpose(0, 3, 1, 2, 4),
            k_new[:, TP:].reshape(L, NB, TB, HA, DH), v_new[:, TP:].reshape(L, NB, TB, HA, DH))
```
